# Optimizing a Trainium2 kernel written in Bass

```python
import jax, jax.numpy as jnp
from jax import lax
import numpy as np

D_MODEL = 1024
BATCH = 1
SEQ = 1024
DEPTH = 1
DEC_BATCH = 8
DEC_SEQ = 16
PAST_LEN = 512

CHUNK = 64
Q_BLOCK = 128
EPS = 1e-6
D_FF = 2816
MLA_HEADS = 8
Q_LORA = 384
KV_LORA = 256
NOPE_DIM = 64
ROPE_DIM = 32
MLA_V_DIM = 64
ROPE_THETA = 10000.0
FOX_HEADS = 8
FOX_HEAD_DIM = 64
FOX_W = FOX_HEADS * FOX_HEAD_DIM
MIX_W = MLA_HEADS * MLA_V_DIM + FOX_W
IN_COLS = Q_LORA + KV_LORA + ROPE_DIM + 3 * FOX_W + FOX_HEADS

kernel_name = "mla_fox_macaron_streaming_step"

def _rmsnorm(x, g):
    x32 = x.astype(jnp.float32)
    y = x32 * lax.rsqrt(jnp.mean(x32 * x32, axis=-1, keepdims=True) + EPS)
    return (y * g.astype(jnp.float32)).astype(x.dtype)

def _swiglu(x, w_gu, w_down):
    gate, up = jnp.split(x @ w_gu, 2, axis=-1)
    return (jax.nn.silu(gate) * up) @ w_down

def _rope(x, pos):
    half = x.shape[-1] // 2
    freqs = ROPE_THETA ** (-jnp.arange(half, dtype=jnp.float32) / half)
    ang = pos.astype(jnp.float32)[:, None] * freqs[None, :]
    cos = jnp.cos(ang)[None, :, None, :]
    sin = jnp.sin(ang)[None, :, None, :]
    x1 = x[..., :half].astype(jnp.float32)
    x2 = x[..., half:].astype(jnp.float32)
    out = jnp.concatenate([x1 * cos - x2 * sin, x1 * sin + x2 * cos], axis=-1)
    return out.astype(x.dtype)

def _attend(q, k, v, q_pos, k_pos, per_frame, lq=None, lk=None):
    B, Tq, H, dk = q.shape
    qb = Q_BLOCK if Tq % Q_BLOCK == 0 else Tq
    nb = Tq // qb
    scale = dk ** -0.5
    k_chunk = k_pos // CHUNK
    decay = lq is not None
    lk_t = jnp.swapaxes(lk, 1, 2)[:, :, None, :] if decay else None

    def block(xs):
        qi, pi = xs[0], xs[1]
        s = jnp.einsum('bqhd,bkhd->bhqk', qi, k, preferred_element_type=jnp.float32) * scale
        if per_frame:
            mask = k_pos[None, :] <= pi[:, None]
        else:
            mask = k_chunk[None, :] <= (pi // CHUNK)[:, None]
        if decay:
            li = jnp.swapaxes(xs[2], 1, 2)[..., None]
            s = s + (li - lk_t)
        s = jnp.where(mask[None, None], s, -jnp.inf)
        p = jax.nn.softmax(s, axis=-1)
        return jnp.einsum('bhqk,bkhd->bqhd', p.astype(v.dtype), v)

    xs = (jnp.swapaxes(q.reshape(B, nb, qb, H, dk), 0, 1), q_pos.reshape(nb, qb))
    if decay:
        xs = xs + (jnp.swapaxes(lq.reshape(B, nb, qb, H), 0, 1),)
    o = lax.map(block, xs)
    return jnp.swapaxes(o, 0, 1).reshape(B, Tq, H, v.shape[-1])

def _token_mix(u, q_pos, past, w_in, b_forget, g_q_latent, w_q_up, g_kv_latent, w_kv_up, w_out):
    B, T, _ = u.shape
    proj = u @ w_in
    sizes = (Q_LORA, KV_LORA, ROPE_DIM, FOX_W, FOX_W, FOX_W, FOX_HEADS)
    idx = np.cumsum(sizes)[:-1].tolist()
    c_q, c_kv, k_rope, f_q, f_k, f_v, f_gate = jnp.split(proj, idx, axis=-1)

    q = (_rmsnorm(c_q, g_q_latent) @ w_q_up).reshape(B, T, MLA_HEADS, NOPE_DIM + ROPE_DIM)
    q = jnp.concatenate([q[..., :NOPE_DIM], _rope(q[..., NOPE_DIM:], q_pos)], axis=-1)
    c_kv = _rmsnorm(c_kv, g_kv_latent)
    k_rope = _rope(k_rope[:, :, None, :], q_pos)[:, :, 0, :]

    f_q = f_q.reshape(B, T, FOX_HEADS, FOX_HEAD_DIM)
    f_k = f_k.reshape(B, T, FOX_HEADS, FOX_HEAD_DIM)
    f_v = f_v.reshape(B, T, FOX_HEADS, FOX_HEAD_DIM)
    logf = jax.nn.log_sigmoid(f_gate.astype(jnp.float32) + b_forget.astype(jnp.float32))

    new_rows = (c_kv, k_rope, f_k, f_v, logf)
    if past is None:
        ckv_all, krope_all, fk_all, fv_all, logf_all = new_rows
        k_pos = q_pos
    else:
        p_ckv, p_krope, p_fk, p_fv, p_logf = past
        ckv_all = jnp.concatenate([p_ckv, c_kv], axis=1)
        krope_all = jnp.concatenate([p_krope, k_rope], axis=1)
        fk_all = jnp.concatenate([p_fk, f_k], axis=1)
        fv_all = jnp.concatenate([p_fv, f_v], axis=1)
        logf_all = jnp.concatenate([p_logf.astype(jnp.float32), logf], axis=1)
        k_pos = jnp.arange(ckv_all.shape[1])
    Tk = ckv_all.shape[1]

    kv = (ckv_all @ w_kv_up).reshape(B, Tk, MLA_HEADS, NOPE_DIM + MLA_V_DIM)
    k_mla = jnp.concatenate(
        [kv[..., :NOPE_DIM], jnp.broadcast_to(krope_all[:, :, None, :], (B, Tk, MLA_HEADS, ROPE_DIM))], axis=-1)
    o_mla = _attend(q, k_mla, kv[..., NOPE_DIM:], q_pos, k_pos, per_frame=False)

    lk = jnp.cumsum(logf_all, axis=1)
    lq = lk[:, Tk - T:]
    o_fox = _attend(f_q, fk_all, fv_all, q_pos, k_pos, True, lq, lk)

    o = jnp.concatenate([o_mla.reshape(B, T, -1), o_fox.reshape(B, T, -1)], axis=-1) @ w_out
    return o, new_rows

def setup_inputs(seed: int = 0) -> dict:
    key = jax.random.key(seed)
    ks = jax.random.split(key, 32)
    f32 = jnp.float32

    def nrm(k, shape, scale=1.0):
        return jax.random.normal(k, shape, f32) * scale

    def gain(k, n):
        return 1.0 + 0.02 * jax.random.normal(k, (DEPTH, n), f32)

    return {
        "x_prompt": nrm(ks[0], (BATCH, SEQ, D_MODEL)),
        "x_sample": nrm(ks[1], (DEC_BATCH, DEC_SEQ, D_MODEL)),
        "cache_mla_ckv": nrm(ks[2], (DEPTH, DEC_BATCH, PAST_LEN, KV_LORA)),
        "cache_mla_krope": nrm(ks[3], (DEPTH, DEC_BATCH, PAST_LEN, ROPE_DIM)),
        "cache_fox_k": nrm(ks[4], (DEPTH, DEC_BATCH, PAST_LEN, FOX_HEADS, FOX_HEAD_DIM)),
        "cache_fox_v": nrm(ks[5], (DEPTH, DEC_BATCH, PAST_LEN, FOX_HEADS, FOX_HEAD_DIM)),
        "cache_fox_logf": jax.nn.log_sigmoid(3.0 + nrm(ks[6], (DEPTH, DEC_BATCH, PAST_LEN, FOX_HEADS))),
        "g_ffn1_pre": gain(ks[7], D_MODEL),
        "g_ffn1_post": gain(ks[8], D_MODEL),
        "w_ffn1_gu": nrm(ks[9], (DEPTH, D_MODEL, 2 * D_FF), D_MODEL ** -0.5),
        "w_ffn1_down": nrm(ks[10], (DEPTH, D_FF, D_MODEL), D_FF ** -0.5),
        "g_mix_pre": gain(ks[11], D_MODEL),
        "g_mix_post": gain(ks[12], D_MODEL),
        "w_in": nrm(ks[13], (DEPTH, D_MODEL, IN_COLS), D_MODEL ** -0.5),
        "b_forget": 3.0 + 0.1 * nrm(ks[14], (DEPTH, FOX_HEADS)),
        "g_q_latent": gain(ks[15], Q_LORA),
        "w_q_up": nrm(ks[16], (DEPTH, Q_LORA, MLA_HEADS * (NOPE_DIM + ROPE_DIM)), Q_LORA ** -0.5),
        "g_kv_latent": gain(ks[17], KV_LORA),
        "w_kv_up": nrm(ks[18], (DEPTH, KV_LORA, MLA_HEADS * (NOPE_DIM + MLA_V_DIM)), KV_LORA ** -0.5),
        "w_out": nrm(ks[19], (DEPTH, MIX_W, D_MODEL), MIX_W ** -0.5),
        "g_ffn2_pre": gain(ks[20], D_MODEL),
        "g_ffn2_post": gain(ks[21], D_MODEL),
        "w_ffn2_gu": nrm(ks[22], (DEPTH, D_MODEL, 2 * D_FF), D_MODEL ** -0.5),
        "w_ffn2_down": nrm(ks[23], (DEPTH, D_FF, D_MODEL), D_FF ** -0.5),
    }

def reference(x_prompt, x_sample, cache_mla_ckv, cache_mla_krope, cache_fox_k, cache_fox_v, cache_fox_logf,
              g_ffn1_pre, g_ffn1_post, w_ffn1_gu, w_ffn1_down, g_mix_pre, g_mix_post, w_in, b_forget,
              g_q_latent, w_q_up, g_kv_latent, w_kv_up, w_out, g_ffn2_pre, g_ffn2_post, w_ffn2_gu, w_ffn2_down):
    past_len = cache_mla_ckv.shape[2]
    pos_p = jnp.arange(x_prompt.shape[1])
    pos_s = past_len + jnp.arange(x_sample.shape[1])

    xp, xs = x_prompt, x_sample
    rows_p, rows_s = [], []
    for l in range(DEPTH):
        def layer(x, pos, past):
            h = x + 0.5 * _rmsnorm(
                _swiglu(_rmsnorm(x, g_ffn1_pre[l]), w_ffn1_gu[l], w_ffn1_down[l]), g_ffn1_post[l])
            mix, rows = _token_mix(_rmsnorm(h, g_mix_pre[l]), pos, past, w_in[l], b_forget[l],
                                   g_q_latent[l], w_q_up[l], g_kv_latent[l], w_kv_up[l], w_out[l])
            h = h + _rmsnorm(mix, g_mix_post[l])
            h = h + 0.5 * _rmsnorm(
                _swiglu(_rmsnorm(h, g_ffn2_pre[l]), w_ffn2_gu[l], w_ffn2_down[l]), g_ffn2_post[l])
            return h, rows

        xp, rp = layer(xp, pos_p, None)
        xs, rs = layer(xs, pos_s, (cache_mla_ckv[l], cache_mla_krope[l], cache_fox_k[l],
                                   cache_fox_v[l], cache_fox_logf[l]))
        rows_p.append(rp)
        rows_s.append(rs)

    p_ckv, p_krope, p_fk, p_fv, p_logf = [jnp.stack([r[i] for r in rows_p]) for i in range(5)]
    s_ckv, s_krope, s_fk, s_fv, s_logf = [jnp.stack([r[i] for r in rows_s]) for i in range(5)]
    return (xp, xs, p_ckv, p_krope, p_fk, p_fv, p_logf, s_ckv, s_krope, s_fk, s_fv, s_logf)


_drawn_inputs = setup_inputs


def setup_inputs(seed=0):
    import zlib

    import numpy as np

    out = dict(_drawn_inputs(seed))
    spreads = {}
    factors = {'g_ffn1_pre': 3.283,
     'g_ffn1_post': 4.945,
     'g_mix_post': 11.92,
     'g_q_latent': 8.0,
     'g_kv_latent': 3.02,
     'g_ffn2_pre': 21.505,
     'g_ffn2_post': 34.792,
     'cache_fox_logf': 4.089}
    for name, (base, spread) in spreads.items():
        noise = np.random.default_rng([zlib.crc32(name.encode()), seed]).standard_normal(out[name].shape)
        drawn = base * np.exp(spread * noise) if base else spread * noise
        out[name] = __import__('jax').numpy.asarray(drawn.astype(out[name].dtype))
    for name, factor in factors.items():
        out[name] = (out[name] * factor).astype(out[name].dtype)
    return out
```

```python
import numpy as np
import concourse.bass as bass
from concourse import mybir
from contextlib import ExitStack

F32, F32R, BF16 = mybir.dt.float32, mybir.dt.float32r, mybir.dt.bfloat16
ACT, ALU, AX = mybir.ActivationFunctionType, mybir.AluOpType, mybir.AxisListType

P = 128
D = 1024
KD = D // P
SEQ, DECB, DECT, PAST = 1024, 8, 16, 512
T = SEQ + DECB * DECT
TT = T // P
PT = SEQ // P
TG, GN = 3, T // 3
FF = 2816
FC = FF // P
FB = 2
NB = FC // FB
EPS = 1e-6
HALF = 512


class Tools:

    def __init__(self, nc, tag):
        self.nc, self.tag, self.ctx, self.sems = nc, tag, ExitStack(), []

    def __enter__(self):
        return self

    def __exit__(self, *e):
        if self.sems and e[0] is None:
            with self.nc.Block() as block:
                @block.gpsimd
                def _(pool):
                    for s in self.sems:
                        pool.sem_clear(s)
        return self.ctx.__exit__(*e)

    def sb(self, name, shape, dt=F32):
        return self.ctx.enter_context(self.nc.sbuf_tensor(f"{self.tag}_{name}", shape, dt))

    def ps(self, name, shape, dt=F32):
        return self.ctx.enter_context(self.nc.psum_tensor(f"{self.tag}_{name}", shape, dt))

    def sem(self, name):
        self.sems.append(self.ctx.enter_context(self.nc.semaphore(f"{self.tag}_{name}")))
        return self.sems[-1]

    def block(self):
        return self.nc.Block()


def plain(ap):
    return ap.bitcast(F32)


def split_product(pe, out, w_hi, w_lo, x_hi, x_lo, first, last):
    pe.matmul(out, w_hi, x_hi, start=first, stop=False)
    pe.matmul(out, w_hi, x_lo, start=False, stop=False)
    return pe.matmul(out, w_lo, x_hi, start=False, stop=last)


class Region:

    def __init__(self, nc, tag, start, size):
        self.nc, self.tag, self.at, self.end = nc, tag, start, start + size

    def take(self, name, shape, dt=F32):
        size = int(np.prod(shape[1:])) * 4
        assert self.at + size <= self.end
        part = self.nc.alloc_sbuf_tensor_at(f"{self.tag}_{name}", shape, dt, offset=self.at)
        self.at += size
        return part


class Boundary:

    def __init__(self, k, name, acc, acc_ready, ident, xT_hi, xT_lo, post, pre, buffers, flips):
        self.acc, self.acc_ready, self.ident, self.xT_hi, self.xT_lo = acc, acc_ready, ident, xT_hi, xT_lo
        self.post, self.pre, self.flips = post, pre, flips
        self.gain, self.resid, self.normed_rows, self.junk = [
            [buffers[i].take(f"{name}_{what}{m}", [P, D])[:, :] for m in range(2)] for i, what in enumerate(("gain", "resid", "normed", "junk"))]
        self.lag = 2 if post else 0
        self.steps = TT + (self.lag + 2 if pre else 0)
        stats = k.sb(f"{name}_stats", [P, 4, 2, TT])
        self.ssq, self.mean, self.root, self.rstd = [stats[:, n, :, :] for n in range(4)]
        self.gain_in = [k.sem(f"{name}_gain_in{m}") for m in range(2)]
        self.resid_in = [k.sem(f"{name}_resid_in{m}") for m in range(2)]
        self.squared, self.mean_ok, self.root_ok, self.rstd_ok, self.normed = [
            [k.sem(f"{name}_{n}_{m}") for m in ("post", "pre")] for n in ("squared", "mean_ok", "root_ok", "rstd_ok", "normed")]
        self.summed, self.stored, self.flipped, self.hi_ok, self.lo_ok = [k.sem(f"{name}_{n}") for n in ("summed", "stored", "flipped", "hi_ok", "lo_ok")]

    def stages(self, s):
        return [(m, t) for m, t, on in ((0, s, self.post), (1, s - self.lag, self.pre)) if on and 0 <= t < TT]

    def load_first(self, sp):
        if self.post:
            sp.dma_start(self.gain[0], self.post[0].partition_broadcast(P)).then_inc(self.gain_in[0], 16)
            for t in range(2):
                sp.dma_start(self.resid[t], self.post[2](t)).then_inc(self.resid_in[t], 16)
        if self.pre is not None:
            sp.dma_start(self.gain[1], self.pre.partition_broadcast(P)).then_inc(self.gain_in[1], 16)

    def load_and_store(self, sp):
        for t in range(TT):
            sp.wait_ge(self.summed, t + 1)
            sp.dma_start(self.post[3](t), self.acc[:, t, :]).then_inc(self.stored, 16)
            if t + 2 < TT:
                sp.dma_start(self.resid[t % 2], self.post[2](t + 2)).then_inc(self.resid_in[t % 2], 16)
        sp.wait_ge(self.stored, 16 * TT)

    def act(self, act, s):
        for m, t in self.stages(s):
            if m == 1 and self.post:
                act.wait_ge(self.summed, t + 1)
            else:
                self.acc_ready(act, t)
            if t:
                act.wait_ge(self.squared[m], t)
            act.activation(self.junk[m], self.acc[:, t, :], ACT.Square, accum_out=self.ssq[:, m, t:t + 1]).then_inc(self.squared[m], 1)
        for m, t in self.stages(s):
            act.wait_ge(self.mean_ok[m], t + 1)
            act.activation(self.root[:, m, t:t + 1], self.mean[:, m, t:t + 1], ACT.Sqrt).then_inc(self.root_ok[m], 1)
        t = s - self.lag - 1
        if self.pre is not None and 0 <= t < TT:
            for h in range(2):
                act.wait_ge(self.flipped, 2 * t + h + 1)
                act.activation(self.xT_hi[:, 4 * h:4 * h + 4, t * P:t * P + P], self.flips[(2 * t + h) % 4].rearrange("p (k n) -> p k n", k=4),
                               ACT.Copy).then_inc(self.hi_ok, 1)

    def dve(self, dve, s):
        for m, t in self.stages(s):
            factor = 1.0 if m else self.post[1]
            dve.wait_ge(self.squared[m], t + 1)
            dve.tensor_scalar(self.mean[:, m, t:t + 1], self.ssq[:, m, t:t + 1], 1.0 / (D * factor ** 2), EPS / factor ** 2, ALU.mult, ALU.add).then_inc(self.mean_ok[m], 1)
        t = s - self.lag - 2
        if self.pre is not None and 0 <= t < TT:
            for h in range(2):
                cols = slice(t * P, t * P + P)
                dve.wait_ge(self.hi_ok, 2 * t + h + 1)
                dve.tensor_tensor(self.xT_lo[:, 4 * h:4 * h + 4, cols], self.flips[(2 * t + h) % 4].rearrange("p (k n) -> p k n", k=4),
                                  plain(self.xT_hi[:, 4 * h:4 * h + 4, cols]), ALU.subtract).then_inc(self.lo_ok, 1)
        for m, t in self.stages(s):
            dve.wait_ge(self.root_ok[m], t + 1)
            dve.reciprocal(self.rstd[:, m, t:t + 1], self.root[:, m, t:t + 1]).then_inc(self.rstd_ok[m], 1)
        for m, t in self.stages(s):
            if t == 0:
                dve.wait_ge(self.gain_in[m], 16)
            if m and t >= 2:
                dve.wait_ge(self.flipped, 2 * (t - 2) + 2)
            dve.wait_ge(self.rstd_ok[m], t + 1)
            dst = self.normed_rows[t % 2] if m else self.acc[:, t, :]
            dve.scalar_tensor_tensor(dst, self.acc[:, t, :], self.rstd[:, m, t:t + 1], self.gain[m], ALU.mult, ALU.mult).then_inc(self.normed[m], 1)

    def pool(self, pool, t):
        pool.wait_ge(self.normed[0], t + 1)
        pool.wait_ge(self.resid_in[t % 2], 16 * (t // 2 + 1))
        pool.tensor_tensor(self.acc[:, t, :], self.acc[:, t, :], self.resid[t % 2], ALU.add).then_inc(self.summed, 1)

    def pe(self, pe, t):
        pe.wait_ge(self.normed[1], t + 1)
        for h in range(2):
            if t >= 2:
                pe.wait_ge(self.lo_ok, 2 * (t - 2) + h + 1)
            for c in range(4):
                kk = 4 * h + c
                last = pe.transpose(self.flips[(2 * t + h) % 4][:, c * P:c * P + P], self.normed_rows[t % 2][:, kk * P:kk * P + P], self.ident[:, :])
            last.then_inc(self.flipped, 1)


def feed_forward(nc, tag, ident, acc, xT_hi, xT_lo, w_gu, w_down, rows_of, entry_post, entry_pre, exit_post, exit_pre):
    with Tools(nc, tag) as k:
        starts = {}

        def buffer(name, shape, dt=F32):
            starts[name] = nc.sbuf_base
            return k.sb(name, shape, dt)

        def borrowed(*names):
            return [Region(nc, tag, starts[name], 2 * D * 4) for name in names]

        gu_raw = [buffer(f"gu_raw{j}", [P, KD, 2 * P]) for j in range(FB)]
        gu_hi = [buffer(f"gu_hi{j}", [P, KD, 2 * P], F32R) for j in range(FB)]
        gu_lo = [buffer(f"gu_lo{j}", [P, KD, 2 * P], F32R) for j in range(FB)]
        dn_raw = buffer("dn_raw", [P, FB, D])
        dn_hi = buffer("dn_hi", [P, FB, D], F32R)
        dn_lo = buffer("dn_lo", [P, FB, D], F32R)
        a_hi = buffer("a_hi", [P, FB, T], F32R)
        a_lo = buffer("a_lo", [P, FB, T], F32R)
        silu = k.sb("silu", [P, 2, GN])
        prod = k.sb("prod", [P, 2, GN])
        gate_ps = k.ps("gate_ps", [P, 2, HALF])
        up_ps = k.ps("up_ps", [P, 2, HALF])
        DR = 3
        down_ps = k.ps("down_ps", [P, DR + 1, HALF])
        gu_in = [k.sem(f"gu_in{j}") for j in range(FB)]
        dn_in = k.sem("dn_in")
        hi_ok = k.sem("hi_ok")
        W = FB + 1
        lo_ok = k.sem("lo_ok")
        GU = FB * TG
        gu_ready = k.sem("gu_ready")
        silu_ok = k.sem("silu_ok")
        prod_ok = k.sem("prod_ok")
        a_hi_ok = k.sem("a_hi_ok")
        a_lo_ok = k.sem("a_lo_ok")
        DU = TT * 2
        down_ready = k.sem("down_ready")
        added = k.sem("added")
        row_in = [k.sem(f"row_in{t}") for t in range(TT if rows_of else 0)]
        gu_src = w_gu.rearrange("(k p) (s f n) -> p k s f n", p=P, s=2, n=P)
        dn_src = w_down.rearrange("(f p) n -> p f n", p=P)
        LAST = NB - 1

        def row_there(act, t):
            if rows_of:
                act.wait_ge(row_in[t], 16)

        def row_summed(act, t):
            act.wait_ge(added, LAST * DU + (DR + 2 * t + 2))

        entry = Boundary(k, "entry", acc, row_there, ident, xT_hi, xT_lo, entry_post, entry_pre,
                         borrowed("dn_hi", "dn_lo", "a_hi", "a_lo"),
                         [down_ps[:, n, :] for n in range(4)])
        leave = Boundary(k, "exit", acc, row_summed, ident, xT_hi, xT_lo, exit_post, exit_pre,
                         borrowed("gu_raw0", "gu_raw1", "gu_hi0", "gu_hi1"),
                         [gate_ps[:, 0, :], gate_ps[:, 1, :], up_ps[:, 0, :], up_ps[:, 1, :]])

        with k.block() as block:
            @block.sync
            def _(sp):
                def gate_up(i, ahead, j):
                    sp.wait_ge(lo_ok, i * W + (ahead * W + j + 1))
                    for s in range(2):
                        at = bass.ds(i * FB + (ahead * FB + j), 1)
                        sp.dma_start(gu_raw[j][:, :, s * P:s * P + P], gu_src[:, :, s, at, :].rearrange("p k f n -> p (k f) n")).then_inc(gu_in[j], 16)

                def down(i, ahead):
                    sp.wait_ge(lo_ok, i * W + (ahead * W + W))
                    sp.dma_start(dn_raw[:, :, :], dn_src[:, bass.ds(i * FB + ahead * FB, FB), :]).then_inc(dn_in, 16)

                if rows_of:
                    for t in range(TT):
                        sp.dma_start(acc[:, t, :], rows_of(t)).then_inc(row_in[t], 16)
                        if t == 0:
                            entry.load_first(sp)
                        if t in (1, 4):
                            gate_up(0, 0, t // 3)
                else:
                    entry.load_first(sp)
                    for j in range(FB):
                        gate_up(0, 0, j)
                down(0, 0)
                if entry.post:
                    entry.load_and_store(sp)
                with sp.Fori(0, LAST) as i:
                    for j in range(FB):
                        gate_up(i, 1, j)
                    down(i, 1)
                sp.wait_ge(lo_ok, LAST * W + (W + FB))
                leave.load_first(sp)
                leave.load_and_store(sp)

            @block.gpsimd
            def _(pool):
                def gate_up(i, ahead, j):
                    pool.wait_ge(hi_ok, i * W + (ahead * W + j + 1))
                    pool.tensor_tensor(gu_lo[j][:, :, :], gu_raw[j][:, :, :], plain(gu_hi[j][:, :, :]), ALU.subtract).then_inc(lo_ok, 1)

                def down(i):
                    pool.wait_ge(hi_ok, i * W + W)
                    pool.tensor_tensor(dn_lo[:, :, :], dn_raw[:, :, :], plain(dn_hi[:, :, :]), ALU.subtract).then_inc(lo_ok, 1)

                pool.sem_inc(lo_ok, W)
                for s in range(TT):
                    if s in (1, 3):
                        gate_up(0, 0, s // 2)
                    if entry.post:
                        entry.pool(pool, s)
                with pool.Fori(0, LAST) as i:
                    down(i)
                    for j in range(FB):
                        gate_up(i, 1, j)
                down(LAST)
                for s in range(TT):
                    leave.pool(pool, s)

            @block.scalar
            def _(act):
                def gate_up(i, ahead, j):
                    act.wait_ge(gu_in[j], i * 32 + (ahead * 32 + 32))
                    act.wait_ge(gu_ready, i * GU + (ahead * GU + TG * (j + 1)))
                    act.activation(gu_hi[j][:, :, :], gu_raw[j][:, :, :], ACT.Copy).then_inc(hi_ok, 1)

                def units(i):
                    for j in range(FB):
                        for g in range(TG):
                            u = j * TG + g
                            act.wait_ge(gu_ready, i * GU + (GU + u + 1))
                            act.activation(silu[:, u % 2, :], gate_ps[:, u % 2, 0:GN], ACT.Silu).then_inc(silu_ok, 1)
                            act.wait_ge(prod_ok, i * GU + (2 + u + 1))
                            act.activation(a_hi[:, j, g * GN:g * GN + GN], prod[:, u % 2, :], ACT.Copy).then_inc(a_hi_ok, 1)
                        if j == 0:
                            act.wait_ge(dn_in, i * 16 + 16)
                            act.wait_ge(down_ready, i * DU + 1)
                            act.activation(dn_hi[:, :, :], dn_raw[:, :, :], ACT.Copy).then_inc(hi_ok, 1)

                for s in range(entry.steps):
                    entry.act(act, s)
                    if s in (1, 3):
                        gate_up(0, 0, s // 2)
                with act.Fori(0, LAST) as i:
                    units(i)
                    for j in range(FB):
                        gate_up(i, 1, j)
                units(LAST)
                for s in range(leave.steps):
                    leave.act(act, s)

            @block.vector
            def _(dve):
                def units(i):
                    for j in range(FB):
                        for g in range(TG):
                            u = j * TG + g
                            dve.wait_ge(silu_ok, i * GU + (u + 1))
                            dve.tensor_tensor(prod[:, u % 2, :], up_ps[:, u % 2, 0:GN], silu[:, u % 2, :], ALU.mult).then_inc(prod_ok, 1)
                            dve.wait_ge(a_hi_ok, i * GU + (u + 1))
                            dve.tensor_tensor(a_lo[:, j, g * GN:g * GN + GN], prod[:, u % 2, :], plain(a_hi[:, j, g * GN:g * GN + GN]),
                                              ALU.subtract).then_inc(a_lo_ok, 1)

                def down(i, t, first=False):
                    for h in range(2):
                        m = 2 * t + h
                        dst = acc[:, t, h * HALF:h * HALF + HALF]
                        dve.wait_ge(down_ready, i * DU + (1 + m + 1))
                        if first:
                            dve.tensor_copy(dst, down_ps[:, m % DR, :]).then_inc(added, 1)
                        else:
                            dve.tensor_tensor(dst, down_ps[:, m % DR, :], dst, ALU.add).then_inc(added, 1)

                dve.sem_inc(prod_ok, 2)
                dve.sem_inc(added, DR)
                for s in range(entry.steps):
                    entry.dve(dve, s)
                units(0)
                if entry.post:
                    dve.wait_ge(entry.stored, 16 * TT)
                for t in range(TT):
                    down(0, t, True)
                with dve.Fori(1, LAST) as i:
                    units(i)
                    for t in range(TT):
                        down(i, t)
                units(LAST)
                for s in range(leave.steps + 1):
                    if s < TT:
                        down(LAST, s)
                    if s:
                        leave.dve(dve, s - 1)

            @block.tensor
            def _(pe):
                def gate_up(i, j, g):
                    u = j * TG + g
                    if g == 0:
                        pe.wait_ge(lo_ok, i * W + (W + j + 1))
                    pe.wait_ge(prod_ok, i * GU + (u + 1))
                    toks = slice(g * GN, g * GN + GN)
                    for s, bank in enumerate((gate_ps, up_ps)):
                        for kk in range(KD):
                            last = split_product(pe, bank[:, u % 2, 0:GN], gu_hi[j][:, kk, s * P:s * P + P], gu_lo[j][:, kk, s * P:s * P + P],
                                                 xT_hi[:, kk, toks], xT_lo[:, kk, toks], kk == 0, kk == KD - 1)
                    last.then_inc(gu_ready, 1)

                def down(i, t):
                    if t == 0:
                        pe.wait_ge(lo_ok, i * W + (W + W))
                    pe.wait_ge(a_lo_ok, i * GU + ((FB - 1) * TG + t * P // GN + 1))
                    for h in range(2):
                        m = 2 * t + h
                        pe.wait_ge(added, i * DU + (m + 1))
                        for j in range(FB):
                            last = split_product(pe, down_ps[:, m % DR, :], a_hi[:, j, t * P:t * P + P], a_lo[:, j, t * P:t * P + P],
                                                 dn_hi[:, j, h * HALF:h * HALF + HALF], dn_lo[:, j, h * HALF:h * HALF + HALF], j == 0, j == FB - 1)
                        last.then_inc(down_ready, 1)

                def block_products(i, first=False):
                    for j in range(FB):
                        for g in range(TG):
                            if first and j == 0:
                                for t in range(g * TT // TG, (g + 1) * TT // TG):
                                    entry.pe(pe, t)
                                pe.wait_ge(entry.lo_ok, 2 * (g + 1) * TT // TG)
                            gate_up(i, j, g)

                pe.sem_inc(gu_ready, GU)
                pe.sem_inc(down_ready, 1)
                block_products(0, True)
                for t in range(TT):
                    down(0, t)
                with pe.Fori(1, LAST) as i:
                    block_products(i)
                    for t in range(TT):
                        down(i, t)
                block_products(LAST)
                AFTER = 4
                for t in range(TT + AFTER):
                    if t < TT:
                        down(LAST, t)
                    if leave.pre is not None and t >= AFTER:
                        leave.pe(pe, t - AFTER)


QL, KVL, ROPE, NOPE, VD = 384, 256, 32, 64, 64
H = 8
FW = H * 64
QW = NOPE + ROPE
IN_COLS = QL + KVL + ROPE + 3 * FW + H
FOX_AT = QL + KVL + ROPE
GATE_AT = IN_COLS - H
QC, KC = QL // P, KVL // P
KH = KD // 2


def input_projection(nc, tag, w_in, xT_hi, xT_lo, fox_rows, cq, ckv, gate):
    cols = [[(FOX_AT + n * FW, FW)] for n in range(3)] + [[(0, QL), (GATE_AT, H)], [(QL, KVL + ROPE)]]
    width = [sum(w for _, w in c) for c in cols]
    NG = len(cols)
    R = 3
    with Tools(nc, tag) as k:
        raw = [k.sb(f"raw{h}", [P, KH, HALF]) for h in range(2)]
        hi = [k.sb(f"hi{h}", [P, KH, HALF], F32R) for h in range(2)]
        lo = [k.sb(f"lo{h}", [P, KH, HALF], F32R) for h in range(2)]
        stage = k.sb("stage", [P, R, HALF])
        prod = k.ps("prod", [P, R, HALF])
        w_at = [[k.sem(f"w_at{n}{h}") for h in range(2)] for n in range(NG)]
        hi_ok = k.sem("hi_ok")
        lo_ok = k.sem("lo_ok")
        half_used = k.sem("half_used")
        tile_ok = k.sem("tile_ok")
        taken = k.sem("taken")
        stored = [k.sem(f"stored{s}") for s in range(R)]
        src = w_in.rearrange("(k p) n -> p k n", p=P)

        with k.block() as block:
            @block.sync
            def _(sp):
                def load(n):
                    for h in range(2):
                        if n:
                            sp.wait_ge(lo_ok, 2 * (n - 1) + h + 1)
                        at = 0
                        for c0, w in cols[n]:
                            sp.dma_start(raw[h][:, :, at:at + w], src[:, h * KH:h * KH + KH, c0:c0 + w]).then_inc(w_at[n][h], 16)
                            at += w
                load(0)
                for n in range(NG):
                    if n + 1 < NG:
                        load(n + 1)
                    if n < 3:
                        for t in range(TT):
                            sp.wait_ge(taken, R + n * TT + t + 1)
                            sp.dma_start(fox_rows[n, t * P:t * P + P, :], stage[:, t % R, :]).then_inc(stored[t % R], 16)
                for s in range(R):
                    sp.wait_ge(stored[s], 3 * TT // R * 16)

            @block.scalar
            def _(act):
                for n in range(NG):
                    for h in range(2):
                        act.wait_ge(w_at[n][h], 16 * len(cols[n]))
                        if n:
                            act.wait_ge(half_used, n) if h == 0 else act.wait_ge(tile_ok, n * TT)
                        act.activation(hi[h][:, :, 0:width[n]], raw[h][:, :, 0:width[n]], ACT.Copy).then_inc(hi_ok, 1)

            @block.gpsimd
            def _(pool):
                for n in range(NG):
                    for h in range(2):
                        pool.wait_ge(hi_ok, 2 * n + h + 1)
                        pool.tensor_tensor(lo[h][:, :, 0:width[n]], raw[h][:, :, 0:width[n]], plain(hi[h][:, :, 0:width[n]]), ALU.subtract).then_inc(lo_ok, 1)

            @block.vector
            def _(dve):
                dve.sem_inc(taken, R)
                for n in range(NG):
                    for t in range(TT):
                        dve.wait_ge(tile_ok, n * TT + t + 1)
                        if n < 3:
                            if n or t >= R:
                                dve.wait_ge(stored[t % R], 16 * (n * TT // R + t // R))
                            dve.tensor_copy(stage[:, t % R, :], prod[:, t % R, :]).then_inc(taken, 1)
                        elif n == 3:
                            dve.tensor_copy(gate[:, t, :], prod[:, t % R, QL:QL + H])
                            dve.tensor_copy(cq[:, t, :], prod[:, t % R, 0:QL]).then_inc(taken, 1)
                        else:
                            dve.tensor_copy(ckv[:, t, :], prod[:, t % R, 0:KVL + ROPE]).then_inc(taken, 1)

            @block.tensor
            def _(pe):
                def group(n, w):
                    for t in range(TT):
                        pe.wait_ge(taken, n * TT + (t + 1))
                        for h in range(2):
                            if t == 0:
                                pe.wait_ge(lo_ok, n * 2 + (h + 1))
                            for kk in range(KH):
                                c = h * KH + kk
                                last = split_product(pe, prod[:, t % R, 0:w], xT_hi[:, c, t * P:t * P + P], xT_lo[:, c, t * P:t * P + P],
                                                     hi[h][:, kk, 0:w], lo[h][:, kk, 0:w], c == 0, c == KD - 1)
                            if t == TT - 1 and h == 0:
                                last.then_inc(half_used, 1)
                        last.then_inc(tile_ok, 1)

                with pe.Fori(0, 3) as n:
                    group(n, HALF)
                for n in range(3, NG):
                    group(n, width[n])


def latent_norms(nc, tag, ident, cq, ckv, gate, g_q, g_kv, b_forget, cos_sin, cqT_hi, cqT_lo, ckvT_hi, ckvT_lo, krope, logf, ckv_out, krope_out, logf_out):
    with Tools(nc, tag) as k:
        gq_bc, gkv_bc, bf_bc = k.sb("gq_bc", [P, QL]), k.sb("gkv_bc", [P, KVL]), k.sb("bf_bc", [P, H])
        cs = k.sb("cs", [P, TT, 2, ROPE // 2])
        ssq, mean, root, rstd = [k.sb(n, [P, 2, TT]) for n in ("ssq", "mean", "root", "rstd")]
        z, mag, e, lnp = [k.sb(n, [P, TT, H]) for n in ("z", "mag", "e", "lnp")]
        rot = k.sb("rot", [P, TT, 4, ROPE // 2])
        junk = k.ps("junk", [P, 2, HALF])
        flip = k.ps("flip", [P, 4, HALF])
        consts_in, squared, zed, magged, exped, lned, mean_ok, root_ok, rstd_ok, normed, flipped, hi_ok, lo_ok, rotated, roped, gated, stored, low = [
            k.sem(n) for n in ("consts_in", "squared", "zed", "magged", "exped", "lned", "mean_ok", "root_ok", "rstd_ok", "normed", "flipped", "hi_ok",
                               "lo_ok", "rotated", "roped", "gated", "stored", "low")]
        x1, x2 = ckv[:, :, KVL:KVL + ROPE // 2], ckv[:, :, KVL + ROPE // 2:KVL + ROPE]
        with k.block() as block:
            @block.sync
            def _(sp):
                sp.dma_start(gq_bc[:, :], g_q.partition_broadcast(P)).then_inc(consts_in, 16)
                sp.dma_start(gkv_bc[:, :], g_kv.partition_broadcast(P)).then_inc(consts_in, 16)
                sp.dma_start(bf_bc[:, :], b_forget.partition_broadcast(P)).then_inc(consts_in, 16)
                sp.dma_start(cs[:, :, :, :], cos_sin).then_inc(consts_in, 16)
                sp.wait_ge(roped, 2)
                sp.dma_start(krope_out.rearrange("(t p) n -> p t n", p=P), krope[:, :, :]).then_inc(stored, 16)
                sp.wait_ge(gated, 1)
                sp.dma_start(logf_out.rearrange("(t p) n -> p t n", p=P), logf[:, :, :]).then_inc(stored, 16)
                sp.wait_ge(normed, 2 * TT)
                sp.dma_start(ckv_out.rearrange("(t p) n -> p t n", p=P), ckv[:, :, 0:KVL]).then_inc(stored, 16)
                sp.wait_ge(stored, 48)

            @block.scalar
            def _(act):
                for t in range(TT):
                    for s, (rows, w) in enumerate(((cq, QL), (ckv, KVL))):
                        if t:
                            act.wait_ge(squared, 2 * t + s - 1)
                        act.activation(junk[:, s, 0:w], rows[:, t, 0:w], ACT.Square, accum_out=ssq[:, s, t:t + 1]).then_inc(squared, 1)
                act.wait_ge(mean_ok, 1)
                act.activation(root[:, :, :], mean[:, :, :], ACT.Sqrt).then_inc(root_ok, 1)
                act.wait_ge(zed, 1)
                act.activation(mag[:, :, :], z[:, :, :], ACT.Abs).then_inc(magged, 1)
                act.wait_ge(magged, 1)
                act.activation(e[:, :, :], mag[:, :, :], ACT.Exp, scale=-1.0).then_inc(exped, 1)
                act.wait_ge(exped, 1)
                act.activation(lnp[:, :, :], e[:, :, :], ACT.Ln, bias=1.0).then_inc(lned, 1)
                for t in range(TT):
                    for s, (dst, c0, nc_) in enumerate(((cqT_hi, 0, QC), (ckvT_hi, QC, KC))):
                        act.wait_ge(flipped, 2 * t + s + 1)
                        act.activation(dst[:, :, t * P:t * P + P], flip[:, (2 * t + s) % 4, 0:nc_ * P].rearrange("p (k n) -> p k n", n=P), ACT.Copy).then_inc(hi_ok, 1)

            @block.vector
            def _(dve):
                dve.wait_ge(consts_in, 64)
                dve.tensor_tensor(z[:, :, :], gate[:, :, :], bf_bc[:, :].unsqueeze(1).broadcast_to([P, TT, H]), ALU.add).then_inc(zed, 1)
                dve.wait_ge(squared, 2 * TT)
                dve.tensor_scalar(mean[:, 0, :], ssq[:, 0, :], 1.0 / QL, EPS, ALU.mult, ALU.add)
                dve.tensor_scalar(mean[:, 1, :], ssq[:, 1, :], 1.0 / KVL, EPS, ALU.mult, ALU.add).then_inc(mean_ok, 1)
                c, s = cs[:, :, 0, :], cs[:, :, 1, :]
                dve.tensor_tensor(rot[:, :, 0, :], x1, c, ALU.mult)
                dve.tensor_tensor(rot[:, :, 1, :], x2, s, ALU.mult)
                dve.tensor_tensor(rot[:, :, 2, :], x1, s, ALU.mult)
                dve.tensor_tensor(rot[:, :, 3, :], x2, c, ALU.mult).then_inc(rotated, 1)
                dve.wait_ge(rotated, 1)
                dve.tensor_tensor(krope[:, :, 0:ROPE // 2], rot[:, :, 0, :], rot[:, :, 1, :], ALU.subtract).then_inc(roped, 1)
                dve.tensor_tensor(krope[:, :, ROPE // 2:ROPE], rot[:, :, 2, :], rot[:, :, 3, :], ALU.add).then_inc(roped, 1)
                dve.wait_ge(lned, 1)
                dve.scalar_tensor_tensor(logf[:, :, :], z[:, :, :], 0.0, lnp[:, :, :], ALU.min, ALU.subtract).then_inc(gated, 1)
                dve.wait_ge(root_ok, 1)
                dve.reciprocal(rstd[:, :, :], root[:, :, :]).then_inc(rstd_ok, 1)
                dve.wait_ge(rstd_ok, 1)

                def split_low(t):
                    for s, (lo, hi, nc_) in enumerate(((cqT_lo, cqT_hi, QC), (ckvT_lo, ckvT_hi, KC))):
                        dve.wait_ge(hi_ok, 2 * t + s + 1)
                        dve.tensor_tensor(lo[:, :, t * P:t * P + P], flip[:, (2 * t + s) % 4, 0:nc_ * P].rearrange("p (k n) -> p k n", n=P),
                                          plain(hi[:, :, t * P:t * P + P]), ALU.subtract).then_inc(lo_ok, 1)

                for t in range(TT):
                    dve.scalar_tensor_tensor(cq[:, t, :], cq[:, t, :], rstd[:, 0, t:t + 1], gq_bc[:, :], ALU.mult, ALU.mult).then_inc(normed, 1)
                    dve.scalar_tensor_tensor(ckv[:, t, 0:KVL], ckv[:, t, 0:KVL], rstd[:, 1, t:t + 1], gkv_bc[:, :], ALU.mult, ALU.mult).then_inc(normed, 1)
                    if t:
                        split_low(t - 1)
                split_low(TT - 1)

            @block.tensor
            def _(pe):
                for t in range(TT):
                    for s, (rows, nc_) in enumerate(((cq, QC), (ckv, KC))):
                        pe.wait_ge(normed, 2 * t + s + 1)
                        if t >= 2:
                            pe.wait_ge(lo_ok, 2 * t + s - 3)
                        for c in range(nc_):
                            last = pe.transpose(flip[:, (2 * t + s) % 4, c * P:c * P + P], rows[:, t, c * P:c * P + P], ident[:, :])
                        last.then_inc(flipped, 1)


def latent_up(nc, tag, w_q_up, w_kv_up, cos_sin, cqT_hi, cqT_lo, ckvT_hi, ckvT_lo, q_rows, kv_rows, q_raw, kv_raw):
    with Tools(nc, tag) as k:
        cs = k.sb("cs", [P, TT, 2, ROPE // 2])
        q_hi, q_lo = k.sb("q_hi", [P, QC, H * QW], F32R), k.sb("q_lo", [P, QC, H * QW], F32R)
        kv_hi, kv_lo = k.sb("kv_hi", [P, KC, D], F32R), k.sb("kv_lo", [P, KC, D], F32R)
        rot = k.sb("rot", [P, 4, H, ROPE // 2])
        prod = k.ps("prod", [P, 4, HALF])
        w_at = [k.sem(f"w_at{n}") for n in range(3)]
        hi_ok, lo_ok, made, taken, rotated, roped = [k.sem(n) for n in ("hi_ok", "lo_ok", "made", "taken", "rotated", "roped")]
        HQ = H * QW // 2
        units = [("q", t, h) for t in range(TT) for h in range(2)] + [("kv", t, h) for t in range(PT) for h in range(2)]
        with k.block() as block:
            @block.sync
            def _(sp):
                sp.dma_start(q_raw[:, :, :], w_q_up.rearrange("(k p) n -> p k n", p=P)).then_inc(w_at[0], 16)
                sp.dma_start(kv_raw[:, :, :], w_kv_up.rearrange("(k p) n -> p k n", p=P)).then_inc(w_at[1], 16)
                sp.dma_start(cs[:, :, :, :], cos_sin).then_inc(w_at[2], 16)

            @block.scalar
            def _(act):
                act.wait_ge(w_at[0], 16)
                act.activation(q_hi[:, :, :], q_raw[:, :, :], ACT.Copy).then_inc(hi_ok, 1)
                act.wait_ge(w_at[1], 16)
                act.activation(kv_hi[:, :, :], kv_raw[:, :, :], ACT.Copy).then_inc(hi_ok, 1)
                for n, (kind, t, h) in enumerate(units):
                    act.wait_ge(made, n + 1)
                    if kind == "q":
                        act.activation(q_rows[:, t, h * HQ:h * HQ + HQ], prod[:, n % 4, 0:HQ], ACT.Copy).then_inc(taken, 1)
                    else:
                        act.activation(kv_rows[:, t, h * HALF:h * HALF + HALF], prod[:, n % 4, :], ACT.Copy).then_inc(taken, 1)

            @block.gpsimd
            def _(pool):
                pool.wait_ge(hi_ok, 1)
                pool.tensor_tensor(q_lo[:, :, :], q_raw[:, :, :], plain(q_hi[:, :, :]), ALU.subtract).then_inc(lo_ok, 1)
                pool.wait_ge(hi_ok, 2)
                pool.tensor_tensor(kv_lo[:, :, :], kv_raw[:, :, :], plain(kv_hi[:, :, :]), ALU.subtract).then_inc(lo_ok, 1)

            @block.vector
            def _(dve):
                dve.wait_ge(w_at[2], 16)
                for t in range(TT):
                    dve.wait_ge(taken, 2 * t + 2)
                    heads = q_rows[:, t, :].rearrange("p (h n) -> p h n", n=QW)
                    x1, x2 = heads[:, :, NOPE:NOPE + ROPE // 2], heads[:, :, NOPE + ROPE // 2:QW]
                    c = cs[:, t, 0, :].unsqueeze(1).broadcast_to([P, H, ROPE // 2])
                    s = cs[:, t, 1, :].unsqueeze(1).broadcast_to([P, H, ROPE // 2])
                    if t:
                        dve.wait_ge(roped, 2 * t)
                    for n, (x, y) in enumerate(((x1, c), (x2, s), (x1, s), (x2, c))):
                        last = dve.tensor_tensor(rot[:, n, :, :], x, y, ALU.mult)
                    last.then_inc(rotated, 1)
                    dve.wait_ge(rotated, t + 1)
                    dve.tensor_tensor(x1, rot[:, 0, :, :], rot[:, 1, :, :], ALU.subtract).then_inc(roped, 1)
                    dve.tensor_tensor(x2, rot[:, 2, :, :], rot[:, 3, :, :], ALU.add).then_inc(roped, 1)

            @block.tensor
            def _(pe):
                for n, (kind, t, h) in enumerate(units):
                    if n >= 4:
                        pe.wait_ge(taken, n - 3)
                    if (t, h) == (0, 0):
                        pe.wait_ge(lo_ok, 1 if kind == "q" else 2)
                    rows = slice(t * P, t * P + P)
                    if kind == "q":
                        for c in range(QC):
                            last = split_product(pe, prod[:, n % 4, 0:HQ], cqT_hi[:, c, rows], cqT_lo[:, c, rows],
                                                 q_hi[:, c, h * HQ:h * HQ + HQ], q_lo[:, c, h * HQ:h * HQ + HQ], c == 0, c == QC - 1)
                    else:
                        for c in range(KC):
                            last = split_product(pe, prod[:, n % 4, :], ckvT_hi[:, c, rows], ckvT_lo[:, c, rows],
                                                 kv_hi[:, c, h * HALF:h * HALF + HALF], kv_lo[:, c, h * HALF:h * HALF + HALF], c == 0, c == KC - 1)
                    last.then_inc(made, 1)


PAIRS = H // 2
NM = 32 * 3
KROWS = NM + PT
HALVES = SEQ // HALF
HT = HALF // P
CHUNKS = [(h, t, max(h * HALF, t * P)) for h in range(HALVES) for t in range((h + 1) * HT)]
NCH = len(CHUNKS)
LAST_OF_HALF = [max(n for n, c in enumerate(CHUNKS) if c[0] == h) for h in range(HALVES)]
PREP_AT = {0: (0, 1), 1: (2, 3)}
MAX_AT = {2: (0, 1), 3: (2, 3), 4: (4,), 5: (5,), 6: (6,), 7: (7,)}
ROWS_AT = {8: 0, 9: 1}
PREP = 4
PASS = PREP // 2 + 1
assert NCH % 2 == 0 and KROWS <= P and HALVES == 2


def prompt_attention(nc, tag, ident, ident_bf, mask_bf, kdim, scale, load, load_count, stage_head, stage_ops, v_of, o_rows, o_at):
    with Tools(nc, tag) as k:
        q_st = [k.sb(f"q_st{b}", [P, PT, kdim]) for b in range(2)]
        k_st = [k.sb(f"k_st{b}", [P, PT, kdim]) for b in range(2)]
        v_st = [k.sb(f"v_st{b}", [P, PT, VD + 1]) for b in range(2)]
        qT_hi = [k.sb(f"qT_hi{b}", [KROWS, SEQ], F32R) for b in range(2)]
        qT_lo = [k.sb(f"qT_lo{b}", [KROWS, SEQ], F32R) for b in range(2)]
        kT_hi = [k.sb(f"kT_hi{b}", [KROWS, SEQ], F32R) for b in range(2)]
        kT_lo = [k.sb(f"kT_lo{b}", [KROWS, SEQ], F32R) for b in range(2)]
        nmax = [k.sb(f"nmax{b}", [P, PT, PT]) for b in range(2)]
        probs = k.sb("probs", [P, 2, HALF])
        inverse = k.sb("inverse", [P, 2, HALVES, HT])
        rough = k.ps("rough", [P, SEQ])
        turn = k.ps("turn", [P, 2, HALF])
        scores = k.ps("scores", [P, 2, HALF])
        out = k.ps("out", [P, HALVES, HT, P])
        rows_in = k.sem("rows_in")
        cleared = k.sem("cleared")
        staged = k.sem("staged")
        v_staged = k.sem("v_staged")
        prepared = k.sem("prepared")
        prep_hi = k.sem("prep_hi")
        turn_out = [k.sem(f"turn_out{n}") for n in range(2)]
        rough_ready = k.sem("rough_ready")
        max_ok = k.sem("max_ok")
        rows_ready = k.sem("rows_ready")
        s_ready = k.sem("s_ready")
        exp_ok = k.sem("exp_ok")
        pv_ok = k.sem("pv_ok")
        inverse_ok = k.sem("inverse_ok")
        o_taken = k.sem("o_taken")
        CLEARS = 2 * 6

        def prep_parts(b, r):
            st, hi, lo = (q_st, qT_hi, qT_lo) if r % 2 == 0 else (k_st, kT_hi, kT_lo)
            cols = slice(r // 2 * HALF, r // 2 * HALF + HALF)
            return st[b], hi[b][0:kdim, cols], lo[b][0:kdim, cols]

        with k.block() as block:
            @block.sync
            def _(sp):
                load(sp, rows_in)

            @block.gpsimd
            def _(pool):
                for b in range(2):
                    pool.memset(nmax[b][:, :, :], 0.0).then_inc(cleared, 1)
                    pool.memset(v_st[b][:, :, VD:VD + 1], 1.0).then_inc(cleared, 1)
                if load_count:
                    pool.wait_ge(rows_in, load_count * 16)
                with pool.Fori(0, PAIRS) as i:
                    for b in range(2):
                        pool.wait_ge(prepared, i * (2 * PREP) + (b + 1) * PREP)
                        stage_head(pool, i * 2 + b, q_st[b], k_st[b], staged)
                        pool.wait_ge(pv_ok, i * (2 * NCH) + (b + 1) * NCH)
                        pool.tensor_copy(v_st[b][:, :, 0:VD], v_of(i * 2 + b)).then_inc(v_staged, 1)

            @block.scalar
            def _(act):
                def exponent(n, b, s):
                    _, _, c0 = CHUNKS[s]
                    w = HALF - c0 % HALF
                    act.wait_ge(s_ready, n * NCH + (s + 1))
                    act.activation(probs[:, s % 2, 0:w], scores[:, s % 2, 0:w], ACT.Exp).then_inc(exp_ok, 1)

                def preparation(n, b, step):
                    for r in PREP_AT.get(step, ()):
                        _, hi, _ = prep_parts(b, r)
                        act.wait_ge(prepared, n * PREP + (2 * PREP + r + 1))
                        act.activation(hi, turn[0:kdim, r % 2, :], ACT.Copy, scale=scale if r % 2 == 0 else 1.0).then_inc(prep_hi, 1)
                    if step in ROWS_AT:
                        g = ROWS_AT[step]
                        act.wait_ge(rows_ready, n * HALVES + (g + 1))
                        act.activation(qT_hi[b][NM:KROWS, g * HALF:g * HALF + HALF], turn[0:PT, g % 2, :], ACT.Copy).then_inc(turn_out[g % 2], 1)

                def head(n, b, follows):
                    for s in range(NCH):
                        if s + 1 < NCH:
                            exponent(n, b, s + 1)
                        elif follows:
                            exponent(n + 1, 1 - b, 0)
                        if follows:
                            preparation(n + 1, 1 - b, s)

                act.wait_ge(cleared, CLEARS)
                for step in range(NCH):
                    preparation(0, 0, step)
                exponent(0, 0, 0)
                with act.Fori(0, PAIRS - 1) as i:
                    for b in range(2):
                        head(i * 2 + b, b, True)
                for b in range(2):
                    head(H - 2 + b, b, b == 0)

            @block.vector
            def _(dve):
                def preparation(n, b, step):
                    for r in PREP_AT.get(step, ()):
                        _, hi, lo = prep_parts(b, r)
                        dve.wait_ge(prep_hi, n * PREP + (r + 1))
                        dve.scalar_tensor_tensor(lo, turn[0:kdim, r % 2, :], scale if r % 2 == 0 else 1.0, plain(hi), ALU.mult, ALU.subtract).then_inc(turn_out[r % 2], 1)
                    for t in MAX_AT.get(step, ()):
                        at = t % 2 * HALF if t < HT else 0
                        dve.wait_ge(rough_ready, n * PT + (t + 1))
                        dve.tensor_reduce(nmax[b][:, t, t:t + 1], rough[:, at:at + (t + 1) * P], axis=AX.X, op=ALU.max, negate=True).then_inc(max_ok, 1)

                def normalise(n, b, h):
                    dve.wait_ge(pv_ok, n * NCH + (2 * NCH + LAST_OF_HALF[h] + 1))
                    dve.reciprocal(inverse[:, b, h, :].unsqueeze(2), out[:, h, :, VD:VD + 1]).then_inc(inverse_ok, 1)
                    dve.wait_ge(inverse_ok, n * HALVES + (h + 1))
                    dve.tensor_tensor(o_rows[:, h * HT:h * HT + HT, bass.ds(n * VD + o_at, VD)], out[:, h, :, 0:VD],
                                      inverse[:, b, h, :].unsqueeze(2).broadcast_to([P, HT, VD]), ALU.mult).then_inc(o_taken, 1)

                def head(n, b, follows):
                    for s in range(NCH):
                        if follows:
                            preparation(n + 1, 1 - b, s)
                        for h in range(HALVES):
                            if s == min(LAST_OF_HALF[h] + 1, NCH - 1):
                                normalise(n, b, h)

                for b in range(2):
                    for x in (qT_hi, qT_lo, kT_lo, kT_hi):
                        rows = slice(kdim // 32 * 32, KROWS)
                        if x is not kT_hi:
                            dve.memset(plain(x[b][rows, :]), 0.0).then_inc(cleared, 1)
                        else:
                            if NM > rows.start:
                                dve.memset(plain(x[b][rows.start:NM, :]), 0.0)
                            dve.memset(plain(x[b][NM:KROWS, :]), 1.0).then_inc(cleared, 1)
                dve.wait_ge(cleared, CLEARS)
                for step in range(NCH):
                    preparation(0, 0, step)
                with dve.Fori(0, PAIRS - 1) as i:
                    for b in range(2):
                        head(i * 2 + b, b, True)
                for b in range(2):
                    head(H - 2 + b, b, b == 0)

            @block.tensor
            def _(pe):
                pe.sem_inc(prepared, 2 * PREP)
                pe.sem_inc(exp_ok, 2)
                pe.sem_inc(pv_ok, 2 * NCH)
                for free in (*turn_out, max_ok):
                    pe.sem_inc(free, 1)
                pe.sem_inc(o_taken, HALVES)

                def preparation(n, b, step):
                    for r in PREP_AT.get(step, ()):
                        st, _, _ = prep_parts(b, r)
                        if r == 0:
                            pe.wait_ge(staged, n * stage_ops + stage_ops)
                        pe.wait_ge(turn_out[r % 2], n * PASS + (r // 2 + 1))
                        for c in range(HT):
                            last = pe.transpose(turn[0:kdim, r % 2, c * P:c * P + P], st[:, r // 2 * HT + c, :], ident[:, :])
                        last.then_inc(prepared, 1)
                    for t in MAX_AT.get(step, ()):
                        if t == 0:
                            for bank in range(2):
                                pe.wait_ge(turn_out[bank], n * PASS + (1 + PREP // 2))
                        pe.wait_ge(max_ok, n * PT + (1 + (0 if t < 2 else t - 1 if t < HT else t)))
                        at = t % 2 * HALF if t < HT else 0
                        cols = (t + 1) * P
                        for c0 in range(0, cols, HALF):
                            w = min(HALF, cols - c0)
                            diagonal = c0 + w == cols
                            last = pe.matmul(rough[:, at + c0:at + c0 + w], qT_hi[b][0:kdim, t * P:t * P + P], kT_hi[b][0:kdim, c0:c0 + w], start=True, stop=not diagonal)
                            if diagonal:
                                last = pe.matmul(rough[:, at + cols - P:at + cols], ident_bf[:, :], mask_bf, start=False, stop=True)
                        last.then_inc(rough_ready, 1)
                    if step in ROWS_AT:
                        g = ROWS_AT[step]
                        pe.wait_ge(turn_out[g % 2], n * PASS + PASS)
                        pe.wait_ge(max_ok, n * PT + (1 + (g + 1) * HT))
                        for c in range(HT):
                            last = pe.transpose(turn[0:PT, g % 2, c * P:c * P + P], nmax[b][:, g * HT + c, :], ident[:, :])
                        last.then_inc(rows_ready, 1)

                def score(n, b, s):
                    h, t, c0 = CHUNKS[s]
                    w = (h + 1) * HALF - c0
                    if s == 0 or h != CHUNKS[s - 1][0]:
                        pe.wait_ge(turn_out[h % 2], n * PASS + (1 + PASS))
                    pe.wait_ge(exp_ok, n * NCH + (s + 1))
                    diagonal = c0 == t * P
                    last = split_product(pe, scores[:, s % 2, 0:w], kT_hi[b][:, t * P:t * P + P], kT_lo[b][:, t * P:t * P + P],
                                         qT_hi[b][:, c0:c0 + w], qT_lo[b][:, c0:c0 + w], True, not diagonal)
                    if diagonal:
                        last = pe.matmul(scores[:, s % 2, 0:P], mask_bf, ident_bf[:, :], start=False, stop=True)
                    last.then_inc(s_ready, 1)

                def head(n, b, follows):
                    for s, (h, t, c0) in enumerate(CHUNKS):
                        if s + 1 < NCH:
                            score(n, b, s + 1)
                        elif follows:
                            score(n + 1, 1 - b, 0)
                        if follows:
                            preparation(n + 1, 1 - b, s)
                        pe.wait_ge(exp_ok, n * NCH + (2 + s + 1))
                        if t == 0:
                            pe.wait_ge(o_taken, n * HALVES + (h + 1))
                        if s == 0:
                            pe.wait_ge(v_staged, n + 1)
                        for u in range(c0 // P, (h + 1) * HT):
                            last = pe.matmul(out[:, h, u % HT, 0:VD + 1], probs[:, s % 2, u * P - c0:u * P - c0 + P], v_st[b][:, t, :], start=(t == 0 and u == c0 // P), stop=(s in LAST_OF_HALF))
                        last.then_inc(pv_ok, 1)

                pe.wait_ge(cleared, CLEARS)
                for step in range(NCH):
                    preparation(0, 0, step)
                score(0, 0, 0)
                with pe.Fori(0, PAIRS - 1) as i:
                    for b in range(2):
                        head(i * 2 + b, b, True)
                for b in range(2):
                    head(H - 2 + b, b, b == 0)


def mla_prompt(nc, ident, ident_bf, mask_bf, q_rows, kv_rows, krope, o_rows):
    def load(sp, done):
        pass

    def stage(pool, n, q_st, k_st, done):
        pool.tensor_copy(q_st[:, :, :], q_rows[:, 0:PT, bass.ds(n * QW, QW)]).then_inc(done, 1)
        pool.tensor_copy(k_st[:, :, 0:NOPE], kv_rows[:, :, bass.ds(n * (NOPE + VD), NOPE)]).then_inc(done, 1)
        pool.tensor_copy(k_st[:, :, NOPE:QW], krope[:, 0:PT, :]).then_inc(done, 1)

    def v_of(n):
        return kv_rows[:, :, bass.ds(n * (NOPE + VD) + NOPE, VD)]

    prompt_attention(nc, "mla", ident, ident_bf, mask_bf, QW, QW ** -0.5, load, 0, stage, 3, v_of, o_rows, 0)


def fox_prompt(nc, ident, ident_bf, mask_bf, tri, ones, logf, fox_rows, rows, o_rows):
    scale = 64 ** -0.5
    with Tools(nc, "decay") as k:
        q_decay = k.sb("q_decay", [P, PT, H])
        k_decay = k.sb("k_decay", [P, PT, H])
        with Tools(nc, "cumsum") as c:
            cum = c.ps("cum", [P, PT, H])
            summed = c.sem("summed")
            with k.block() as block:
                @block.tensor
                def _(pe):
                    for t in range(PT):
                        for s in range(t):
                            pe.matmul(cum[:, t, :], ones[:, :], logf[:, s, :], start=(s == 0), stop=False)
                        last = pe.matmul(cum[:, t, :], tri[:, :], logf[:, t, :], start=(t == 0), stop=True)
                    last.then_inc(summed, 1)

                @block.vector
                def _(dve):
                    dve.wait_ge(summed, 1)
                    dve.tensor_scalar(q_decay[:, :, :], cum[:, :, :], 1 / scale, None, ALU.mult)
                    dve.tensor_scalar(k_decay[:, :, :], cum[:, :, :], -1.0, None, ALU.mult)

        def load(sp, done):
            for n in range(3):
                sp.dma_start(rows[n][:, :, :], fox_rows[n, 0:SEQ, :].rearrange("(t p) n -> p t n", p=P)).then_inc(done, 16)

        def stage(pool, n, q_st, k_st, done):
            pool.tensor_copy(q_st[:, :, 0:64], rows[0][:, :, bass.ds(n * 64, 64)]).then_inc(done, 1)
            pool.tensor_copy(q_st[:, :, 64:65], q_decay[:, :, bass.ds(n, 1)]).then_inc(done, 1)
            pool.memset(q_st[:, :, 65:66], 1 / scale).then_inc(done, 1)
            pool.tensor_copy(k_st[:, :, 0:64], rows[1][:, :, bass.ds(n * 64, 64)]).then_inc(done, 1)
            pool.memset(k_st[:, :, 64:65], 1.0).then_inc(done, 1)
            pool.tensor_copy(k_st[:, :, 65:66], k_decay[:, :, bass.ds(n, 1)]).then_inc(done, 1)

        def v_of(n):
            return rows[2][:, :, bass.ds(n * VD, VD)]

        prompt_attention(nc, "fox", ident, ident_bf, mask_bf, 66, scale, load, 3, stage, 6, v_of, o_rows, H * VD)


NEW = DECT
CK = PAST // P
KEYS = PAST + NEW
BH = DECB * H
assert BH == 64 and H * NEW == P and PAST % 64 == 0 and NEW <= 64


def sample_setup(nc, ident, q_sample, w_kv_up, select, cache_logf, fox_rows, ckv_out, krope_out, logf_out, s):
    with Tools(nc, "setup") as k:
        logs_in = k.sb("logs_in", [P, DECB, CK, H])
        logs_r = k.sb("logs_r", [P, CK, DECB, H])
        new_logs = k.sb("new_logs", [NEW, DECB, H])
        logs = k.sb("logs", [BH, KEYS])
        ones = k.sb("ones", [BH, KEYS])
        cum = k.sb("cum", [BH, KEYS])
        fq, fk, cn, kn = k.sb("fq", [P, FW]), k.sb("fk", [P, FW]), k.sb("cn", [P, KVL]), k.sb("kn", [P, ROPE])
        qnT = k.sb("qnT", [NOPE, H, P])
        wkT = k.sb("wkT", [NOPE, H, KVL])
        flip = k.ps("flip", [P, 4, HALF])
        rows_in, regrouped, sel_at, flipped, moved, ready, scanned, absorbed = [k.sem(n) for n in ("rows_in", "regrouped", "sel_at", "flipped", "moved", "ready", "scanned", "absorbed")]
        sel_low, sel_high = s["aug_l"][0:BH, :, :], s["aug_l"][BH:P, :, :]


        with k.block() as block:
            @block.sync
            def _(sp):
                sp.dma_start(logs_in[:, :, :, :], cache_logf.rearrange("b (p r) h -> p b r h", r=CK)).then_inc(rows_in, 16)
                tail = slice(SEQ, T)
                sp.dma_start(fq[:, :], fox_rows[0, tail, :]).then_inc(rows_in, 16)
                sp.dma_start(fk[:, :], fox_rows[1, tail, :]).then_inc(rows_in, 16)
                sp.dma_start(cn[:, :], ckv_out[tail, :]).then_inc(rows_in, 16)
                sp.dma_start(kn[:, :], krope_out[tail, :]).then_inc(rows_in, 16)
                sp.dma_start(s["w_kv"][:, :, :], w_kv_up.rearrange("(k p) n -> p k n", p=P)).then_inc(rows_in, 16)
                sp.dma_start(new_logs[:, :, :], logf_out[tail, :].rearrange("(b t) h -> t b h", t=NEW)).then_inc(rows_in, 16)
                sp.dma_start(sel_low, select).then_inc(sel_at, 16)
                sp.dma_start(sel_high, select).then_inc(sel_at, 16)
                sp.wait_ge(sel_at, 32)

            @block.gpsimd
            def _(pool):
                pool.memset(s["qbd"][:, :, :, :], 0.0).then_inc(ready, 1)
                pool.memset(ones[:, :], 1.0).then_inc(ready, 1)

            @block.tensor
            def _(pe):
                pe.wait_ge(rows_in, 112)
                pe.wait_ge(regrouped, 1)
                for r in range(CK):
                    last = pe.transpose(flip[0:BH, 0, r * P:r * P + P], logs_r[:, r, :, :].rearrange("p b h -> p (b h)"), ident[:, :])
                last.then_inc(flipped, 1)
                for n, rows in ((1, fq), (2, fk)):
                    for c in range(4):
                        last = pe.transpose(flip[:, n, c * P:c * P + P], rows[:, c * P:c * P + P], ident[:, :])
                    last.then_inc(flipped, 1)
                for c in range(KC):
                    pe.transpose(flip[:, 3, c * P:c * P + P], cn[:, c * P:c * P + P], ident[:, :])
                pe.transpose(flip[0:ROPE, 3, KVL:KVL + P], kn[:, :], ident[:, :])
                pe.transpose(flip[0:BH, 3, KVL + P:KVL + P + NEW], new_logs[:, :, :].rearrange("t b h -> t (b h)"), ident[0:NEW, 0:NEW]).then_inc(flipped, 1)
                heads = q_sample[:, :].rearrange("p (h n) -> p h n", n=QW)
                for n in range(4, 8):
                    pe.wait_ge(moved, n - 3)
                    for c in range(4):
                        h = (n % 2) * 4 + c
                        if n < 6:
                            last = pe.transpose(flip[0:NOPE, n % 4, c * P:c * P + P], heads[:, h, 0:NOPE], ident[:, :])
                        else:
                            last = pe.transpose(flip[0:ROPE, n % 4, c * P:c * P + P], heads[:, h, NOPE:QW], ident[:, :])
                    last.then_inc(flipped, 1)
                for n in range(8, 12):
                    pe.wait_ge(moved, n - 3)
                    for c in range(4):
                        h = (n - 8) * 2 + c // 2
                        last = pe.transpose(flip[0:NOPE, n % 4, c * P:c * P + P], s["w_kv"][:, c % 2, h * P:h * P + NOPE], ident[:, :])
                    last.then_inc(flipped, 1)
                for n in range(12, 16):
                    pe.wait_ge(moved, 12 if n == 12 else n - 3)
                    c = (n - 12) // 2
                    for i in range(4):
                        h = n % 2 * 4 + i
                        last = pe.matmul(flip[:, n % 4, i * P:i * P + P], wkT[:, h, c * P:c * P + P], qnT[:, h, :], start=True, stop=True)
                    last.then_inc(flipped, 1)

            @block.vector
            def _(dve):
                dve.wait_ge(rows_in, 112)
                dve.tensor_copy(logs_r[:, :, :, :].rearrange("p r b h -> p b r h"), logs_in[:, :, :, :]).then_inc(regrouped, 1)
                dve.wait_ge(flipped, 1)
                dve.tensor_copy(logs[:, 0:PAST].rearrange("q (p r) -> q r p", r=CK), flip[0:BH, 0, :].rearrange("q (r p) -> q r p", r=CK)).then_inc(moved, 1)
                dve.wait_ge(flipped, 2)
                dve.wait_ge(ready, 1)
                for j in range(2):
                    for c in range(4):
                        src = flip[64 * j:64 * j + 64, 1, c * P:c * P + P].rearrange("p (b t) -> p b t", t=NEW)
                        last = dve.tensor_scalar(s["qbd"][64 * j:64 * j + 64, c, :, (2 * c + j) * NEW:(2 * c + j + 1) * NEW], src, 64 ** -0.5, None, ALU.mult)
                last.then_inc(moved, 1)
                dve.wait_ge(flipped, 3)
                dve.tensor_copy(s["knT"][:, :, :], flip[:, 2, :].rearrange("p (c n) -> p c n", c=4)).then_inc(moved, 1)
                dve.wait_ge(flipped, 4)
                dve.tensor_copy(s["cnT"][:, :, :], flip[:, 3, 0:KVL].rearrange("p (c n) -> p c n", c=KC))
                dve.tensor_copy(s["krnT"][:, :], flip[0:ROPE, 3, KVL:KVL + P])
                dve.tensor_copy(logs[:, PAST:KEYS], flip[0:BH, 3, KVL + P:KVL + P + NEW]).then_inc(moved, 1)
                for n in range(4, 8):
                    dve.wait_ge(flipped, n + 1)
                    hs = slice(n % 2 * 4, n % 2 * 4 + 4)
                    if n < 6:
                        dve.tensor_copy(qnT[:, hs, :], flip[0:NOPE, n % 4, :].rearrange("p (h n) -> p h n", h=4)).then_inc(moved, 1)
                    else:
                        dve.tensor_copy(s["qrT"][:, :, hs, :].rearrange("p b h t -> p h b t"), flip[0:ROPE, n % 4, :].rearrange("p (h b t) -> p h b t", h=4, t=NEW)).then_inc(moved, 1)
                for n in range(8, 12):
                    dve.wait_ge(flipped, n + 1)
                    dve.tensor_copy(wkT[:, (n - 8) * 2:(n - 8) * 2 + 2, :], flip[0:NOPE, n % 4, :].rearrange("p (h n) -> p h n", h=2)).then_inc(moved, 1)
                for n in range(12, 16):
                    dve.wait_ge(flipped, n + 1)
                    c, hs = (n - 12) // 2, slice(n % 2 * 4, n % 2 * 4 + 4)
                    dve.tensor_copy(s["qcT"][:, c, :, hs, :].rearrange("p b h t -> p h b t"), flip[:, n % 4, :].rearrange("p (h b t) -> p h b t", h=4, t=NEW)).then_inc(moved, 1)
                dve.wait_ge(ready, 2)
                dve.wait_ge(moved, 16)
                dve.tensor_tensor_scan(cum[:, :], ones[:, :], logs[:, :], 0.0, ALU.mult, ALU.add).then_inc(scanned, 1)
                dve.wait_ge(scanned, 1)
                dve.tensor_scalar(s["aug_r"][0:BH, :], cum[:, :], -1.0, None, ALU.mult)
                dve.memset(s["aug_r"][BH:P, :], 1.0)
                dve.tensor_copy(s["l_new"][BH:P, :], cum[:, PAST:KEYS]).then_inc(scanned, 1)
                dve.wait_ge(scanned, 2)
                dve.wait_ge(sel_at, 32)
                grid = sel_high.rearrange("q b (h t) -> q (b h) t", t=NEW)
                dve.tensor_tensor(grid, grid, s["l_new"][BH:P, :].unsqueeze(1).broadcast_to([BH, BH, NEW]), ALU.mult)


def sample_attention(nc, ident, ident_bf, mask_bf, head_pick, s, cache_ckv, cache_krope, cache_fk, cache_fv, fox_rows, ckv_out, o_rows):
    with Tools(nc, "dec") as k:
        ckv = [k.sb(f"ckv{b}", [P, CK, KVL]) for b in range(2)]
        kr = [k.sb(f"kr{b}", [P, CK, ROPE]) for b in range(2)]
        fk = [k.sb(f"fk{b}", [P, CK, FW]) for b in range(2)]
        fv = [s["fv0"], s["fv1"]]
        cn = [k.sb(f"cn{b}", [NEW, KVL]) for b in range(2)]
        vn = [k.sb(f"vn{b}", [NEW, FW]) for b in range(2)]
        ckvT = [k.sb(f"ckvT{b}", [P, KC, PAST]) for b in range(2)]
        krT = [k.sb(f"krT{b}", [ROPE, PAST]) for b in range(2)]
        fkT = [k.sb(f"fkT{b}", [P, 4, PAST]) for b in range(2)]
        qc = [k.sb(f"qc{b}", [P, KC, P]) for b in range(2)]
        qr = [k.sb(f"qr{b}", [ROPE, P]) for b in range(2)]
        qf = [k.sb(f"qf{b}", [P, 4, P]) for b in range(2)]
        qa = [k.sb(f"qa{b}", [P, P]) for b in range(2)]
        p_sb = [k.sb(f"p_sb{m}", [P, KEYS]) for m in range(2)]
        pT = [k.sb(f"pT{m}", [P, CK, P]) for m in range(2)]
        pTn = [k.sb(f"pTn{m}", [NEW, P]) for m in range(2)]
        nmax, total, inverse = [k.sb(n, [P, 2, 2]) for n in ("nmax", "total", "inverse")]
        picked = k.sb("picked", [P, H, 64])
        folded = k.sb("folded", [P, 64])
        o_mla = k.sb("o_mla", [P, DECB, KVL])
        o_fox = k.sb("o_fox", [P, DECB, 64])
        flip = k.ps("flip", [P, 2, HALF])
        scores = [k.ps(f"scores{m}", [P, 2 * HALF]) for m in range(2)]
        pT_ps = k.ps("pT_ps", [P, HALF])
        o_ps = k.ps("o_ps", [P, HALF])
        cache_in = [k.sem(f"cache_in{b}") for b in range(2)]
        staged = k.sem("staged")
        flip_ready = k.sem("flip_ready")
        flip_ok = [k.sem("flip_ok_act"), k.sem("flip_ok_dve")]
        s_ready = k.sem("s_ready")
        max_ok, exp_ok, pt_ready, pt_ok = [k.sem(n) for n in ("max_ok", "exp_ok", "pt_ready", "pt_ok")]
        pv_ok = k.sem("pv_ok")
        inverse_ok, picked_ok, folded_ok, o_taken = [k.sem(n) for n in ("inverse_ok", "picked_ok", "folded_ok", "o_taken")]
        LOADS, STAGES, FLIPS = 6, 4, 7

        def flips(b):
            out = [([ckv[b][:, r, c * P:c * P + P] for r in range(CK)], ckvT[b][:, c, :], P) for c in range(KC)]
            out += [([kr[b][:, r, :] for r in range(CK)], krT[b][:, :], ROPE)]
            out += [([fk[b][:, r, c * P:c * P + P] for r in range(CK)], fkT[b][:, c, :], P) for c in range(4)]
            return out

        def flip_number(b, g):
            return b * FLIPS + g

        with k.block() as block:
            @block.sync
            def _(sp):
                with sp.Fori(0, DECB // 2) as i:
                    for b in range(2):
                        sp.wait_ge(pv_ok, i * 4 + (2 * b + 2))
                        for dst, src in ((ckv, cache_ckv), (kr, cache_krope), (fk, cache_fk), (fv, cache_fv)):
                            sp.dma_start(dst[b][:, :, :], src[bass.ds(i * 2 + b, 1), :, :].rearrange("b (p r) n -> p (b r) n", r=CK)).then_inc(cache_in[b], 16)
                        new = bass.ds((i * 2 + b) * NEW + SEQ, NEW)
                        sp.dma_start(cn[b][:, :], ckv_out[new, :]).then_inc(cache_in[b], 16)
                        sp.dma_start(vn[b][:, :], fox_rows[2, new, :]).then_inc(cache_in[b], 16)

            @block.gpsimd
            def _(pool):
                with pool.Fori(0, DECB // 2) as i:
                    for b in range(2):
                        n = i * 2 + b
                        pool.wait_ge(s_ready, i * 4 + (2 * b + 2))
                        pool.tensor_copy(qc[b][:, :, :].unsqueeze(2), s["qcT"][:, :, bass.ds(n, 1), :, :].rearrange("p c b h t -> p c b (h t)")).then_inc(staged, 1)
                        pool.tensor_copy(qr[b][:, :].unsqueeze(1), s["qrT"][:, bass.ds(n, 1), :, :].rearrange("p b h t -> p b (h t)")).then_inc(staged, 1)
                        pool.tensor_copy(qf[b][:, :, :].unsqueeze(2), s["qbd"][:, :, bass.ds(n, 1), :]).then_inc(staged, 1)
                        pool.tensor_copy(qa[b][:, :].unsqueeze(1), s["aug_l"][:, bass.ds(n, 1), :]).then_inc(staged, 1)

            def take_flips(eng, copy, parity, i2, b):
                for g, (_, dst, parts) in enumerate(flips(b)):
                    G = flip_number(b, g)
                    if G % 2 == parity:
                        eng.wait_ge(flip_ready, i2 * (2 * FLIPS) + (G + 1))
                        copy(dst, flip[0:parts, parity, :]).then_inc(flip_ok[parity], 1)

            @block.scalar
            def _(act):
                def copy(dst, src):
                    return act.activation(dst, src, ACT.Copy)

                def stream(i, b, follows):
                    n2 = i * 4 + 2 * b
                    for m in range(2):
                        act.wait_ge(max_ok, n2 + (m + 1))
                        act.activation(p_sb[m][:, :], scores[m][:, 0:KEYS], ACT.Exp, bias=nmax[:, b, m:m + 1],
                                       scale=QW ** -0.5 if m == 0 else 1.0, accum_out=total[:, b, m:m + 1]).then_inc(exp_ok, 1)
                    if follows:
                        take_flips(act, copy, 0, i + b, 1 - b)
                    for m in range(2):
                        act.wait_ge(pt_ready, n2 + (m + 1))
                        act.activation(pT[m][:, :, :], pT_ps[:, :].rearrange("p (r n) -> p r n", r=CK), ACT.Copy)
                        act.activation(pTn[m][:, :], scores[m][0:NEW, HALF + P:HALF + 2 * P], ACT.Copy).then_inc(pt_ok, 1)

                take_flips(act, copy, 0, 0, 0)
                with act.Fori(0, DECB // 2 - 1) as i:
                    for b in range(2):
                        stream(i, b, True)
                for b in range(2):
                    stream(DECB // 2 - 1, b, b == 0)

            @block.vector
            def _(dve):
                def stream(i, b, follows):
                    n2 = i * 4 + 2 * b
                    n = i * 2 + b
                    for m in range(2):
                        dve.wait_ge(s_ready, n2 + (4 + m + 1))
                        dve.tensor_reduce(nmax[:, b, m:m + 1], scores[m][:, 0:KEYS], axis=AX.X, op=ALU.max, negate=True).then_inc(max_ok if m else inverse_ok, 1)
                        if m == 0:
                            dve.wait_ge(inverse_ok, n * 2 + 1)
                            dve.tensor_scalar(nmax[:, b, 0:1], nmax[:, b, 0:1], QW ** -0.5, None, ALU.mult).then_inc(max_ok, 1)
                    if follows:
                        take_flips(dve, dve.tensor_copy, 1, i + b, 1 - b)
                    dve.wait_ge(exp_ok, n2 + 2)
                    dve.reciprocal(inverse[:, b, :], total[:, b, :]).then_inc(inverse_ok, 1)
                    dve.wait_ge(inverse_ok, n * 2 + 2)
                    dve.wait_ge(pv_ok, n2 + (4 + 1))
                    dve.tensor_scalar(o_mla[:, bass.ds(n, 1), :], o_ps[:, 0:KVL].unsqueeze(1), inverse[:, b, 0:1], None, ALU.mult).then_inc(o_taken, 1)
                    dve.wait_ge(pv_ok, n2 + (4 + 2))
                    dve.wait_ge(folded_ok, n + 1)
                    dve.tensor_tensor(picked[:, :, :], o_ps[:, :].rearrange("p (h d) -> p h d", h=H), head_pick.unsqueeze(2).broadcast_to([P, H, 64]), ALU.mult).then_inc(o_taken, 1)
                    dve.wait_ge(o_taken, n2 + (1 + 2))
                    dve.tensor_reduce(folded[:, :], picked[:, :, :].rearrange("p h d -> p d h"), axis=AX.X, op=ALU.add).then_inc(picked_ok, 1)
                    dve.wait_ge(picked_ok, n + 1)
                    dve.tensor_scalar(o_fox[:, bass.ds(n, 1), :], folded[:, :].unsqueeze(1), inverse[:, b, 1:2], None, ALU.mult).then_inc(folded_ok, 1)

                take_flips(dve, dve.tensor_copy, 1, 0, 0)
                with dve.Fori(0, DECB // 2 - 1) as i:
                    for b in range(2):
                        stream(i, b, True)
                for b in range(2):
                    stream(DECB // 2 - 1, b, b == 0)

            @block.tensor
            def _(pe):
                pe.sem_inc(s_ready, 4)
                pe.sem_inc(pv_ok, 4)
                for free in (pt_ok, o_taken, folded_ok):
                    pe.sem_inc(free, 1)

                def transpose_caches(i2, b):
                    pe.wait_ge(cache_in[b], i2 * (16 * LOADS) + 16 * LOADS)
                    for g, (rows, _, parts) in enumerate(flips(b)):
                        G = flip_number(b, g)
                        if not isinstance(i2, int) or G // 2:
                            pe.wait_ge(flip_ok[G % 2], i2 * FLIPS + G // 2)
                        for r in range(CK):
                            last = pe.transpose(flip[0:parts, G % 2, r * P:r * P + P], rows[r], ident[:, :])
                        last.then_inc(flip_ready, 1)

                def product(out, pairs, more):
                    for c, (w, x) in enumerate(pairs):
                        last = pe.matmul(out, w, x, start=(c == 0), stop=(c == len(pairs) - 1 and not more))
                    return last

                def stream(i, b, follows):
                    n, n2 = i * 2 + b, i * 4 + 2 * b
                    new = bass.ds(n * NEW, NEW)
                    pe.wait_ge(staged, n * STAGES + STAGES)
                    for e in range(2):
                        pe.wait_ge(flip_ok[e], i * FLIPS + ((FLIPS + 1 - e) // 2 if b == 0 else FLIPS))
                    pe.wait_ge(pt_ok, n2 + 1)
                    product(scores[0][:, 0:PAST], [(qc[b][:, c, :], ckvT[b][:, c, :]) for c in range(KC)] + [(qr[b][:, :], krT[b][:, :])], False)
                    product(scores[0][:, PAST:KEYS], [(qc[b][:, c, :], s["cnT"][:, c, new]) for c in range(KC)] + [(qr[b][:, :], s["krnT"][:, new])], False).then_inc(s_ready, 1)
                    product(scores[1][:, 0:PAST], [(qf[b][:, c, :], fkT[b][:, c, :]) for c in range(4)] + [(qa[b][:, :], s["aug_r"][:, 0:PAST].rearrange("q (p r) -> q r p", r=CK))], False)
                    product(scores[1][:, PAST:KEYS], [(qf[b][:, c, :], s["knT"][:, c, new]) for c in range(4)] + [(qa[b][:, :], s["aug_r"][:, PAST:KEYS])], True)
                    pe.matmul(scores[1][:, PAST:KEYS], ident_bf[:, :], mask_bf, start=False, stop=True).then_inc(s_ready, 1)
                    if follows:
                        transpose_caches(i + b, 1 - b)
                    for m in range(2):
                        pe.wait_ge(exp_ok, n2 + (m + 1))
                        pe.wait_ge(pt_ok, n2 + (1 + m))
                        for r in range(CK):
                            pe.transpose(pT_ps[:, r * P:r * P + P], p_sb[m][:, r * P:r * P + P], ident[:, :])
                        pe.transpose(scores[m][0:NEW, HALF + P:HALF + 2 * P], p_sb[m][:, PAST:KEYS], ident[:, :]).then_inc(pt_ready, 1)
                        pe.wait_ge(pt_ok, n2 + (1 + m + 1))
                        pe.wait_ge(o_taken, n2 + (1 + m))
                        rows, new_rows, w = (ckv[b], cn[b], KVL) if m == 0 else (fv[b], vn[b], FW)
                        for r in range(CK):
                            pe.matmul(o_ps[:, 0:w], pT[m][:, r, :], rows[:, r, :], start=(r == 0), stop=False)
                        pe.matmul(o_ps[:, 0:w], pTn[m][:, :], new_rows[:, :], start=False, stop=True).then_inc(pv_ok, 1)

                transpose_caches(0, 0)
                with pe.Fori(0, DECB // 2 - 1) as i:
                    for b in range(2):
                        stream(i, b, True)
                for b in range(2):
                    stream(DECB // 2 - 1, b, b == 0)

        with Tools(nc, "back") as e:
            olT = fk[0][:, :, :].rearrange("p r n -> p (r n)").rearrange("p (c h b t) -> p c h b t", c=KC, h=H, t=NEW)
            ofT = fk[1][0:64, :, :].rearrange("p r n -> p (r n)")[:, 0:H * P].rearrange("p (h b t) -> p h b t", h=H, t=NEW)
            hop, hopped, rows_ok = e.sem("hop"), e.sem("hopped"), e.sem("rows_ok")
            banks = [flip[:, 0, :], flip[:, 1, :]]
            mla_out, fox_out = pT_ps, o_ps
            units = [(b, m) for b in range(DECB) for m in range(2)]
            with e.block() as block:
                @block.tensor
                def _(pe):
                    for n, (b, m) in enumerate(units):
                        if n >= 2:
                            pe.wait_ge(hopped, n - 1)
                        if m == 0:
                            for c in range(KC):
                                last = pe.transpose(banks[m][:, c * P:c * P + P], o_mla[:, b, c * P:c * P + P], ident[:, :])
                        else:
                            last = pe.transpose(banks[m][0:64, 0:P], o_fox[:, b, :], ident[:, :])
                        last.then_inc(hop, 1)
                    pe.wait_ge(hopped, len(units))
                    for h in range(H):
                        for c in range(KC):
                            pe.matmul(mla_out[:, h * VD:h * VD + VD], olT[:, c, h, :, :].rearrange("p b t -> p (b t)"), s["w_kv"][:, c, h * P + NOPE:h * P + P],
                                      start=(c == 0), stop=(c == KC - 1))
                    for h in range(H):
                        last = pe.transpose(fox_out[:, h * 64:h * 64 + 64], ofT[:, h, :, :].rearrange("p b t -> p (b t)"), ident[0:64, 0:64])
                    last.then_inc(hop, 1)

                @block.vector
                def _(dve):
                    for n, (b, m) in enumerate(units):
                        dve.wait_ge(hop, n + 1)
                        if m == 0:
                            dve.tensor_copy(olT[:, :, :, b, :], banks[m][:, 0:KVL].rearrange("p (c h t) -> p c h t", c=KC, t=NEW)).then_inc(hopped, 1)
                        else:
                            dve.tensor_copy(ofT[:, :, b, :], banks[m][0:64, 0:P].rearrange("p (h t) -> p h t", t=NEW)).then_inc(hopped, 1)
                    dve.wait_ge(hop, len(units) + 1)
                    dve.tensor_copy(o_rows[:, PT, 0:HALF], mla_out[:, :])
                    dve.tensor_copy(o_rows[:, PT, HALF:D], fox_out[:, :])


def output_projection(nc, tag, ident, w_out, xT_hi, xT_lo, acc):
    RAW = 4
    with Tools(nc, tag) as k:
        raw = k.sb("raw", [P, RAW, D])
        hi = k.sb("hi", [P, KD, D], F32R)
        lo = k.sb("lo", [P, KD, D], F32R)
        prod = k.ps("prod", [P, 4, HALF])
        flip = k.ps("flip", [P, 4, HALF])
        w_at = [k.sem(f"w_at{s}") for s in range(RAW)]
        w_lo = [k.sem(f"w_lo_{n}") for n in ("pool", "dve")]
        w_hi, flipped, hi_ok, lo_ok, made, taken = [k.sem(n) for n in ("w_hi", "flipped", "hi_ok", "lo_ok", "made", "taken")]
        src = w_out.rearrange("(k p) n -> p k n", p=P)

        def split_weight(eng, c):
            eng.wait_ge(w_hi, c + 1)
            eng.tensor_tensor(lo[:, c, :], raw[:, c % RAW, :], plain(hi[:, c, :]), ALU.subtract).then_inc(w_lo[c % 2], 1)

        with k.block() as block:
            @block.sync
            def _(sp):
                for c in range(KD):
                    if c >= RAW:
                        sp.wait_ge(w_lo[c % 2], (c - RAW) // 2 + 1)
                    sp.dma_start(raw[:, c % RAW, :], src[:, c, :]).then_inc(w_at[c % RAW], 16)

            @block.scalar
            def _(act):
                def split_high(t):
                    for h in range(2):
                        act.wait_ge(flipped, 2 * t + h + 1)
                        act.activation(xT_hi[:, 4 * h:4 * h + 4, t * P:t * P + P], flip[:, (2 * t + h) % 4, :].rearrange("p (k n) -> p k n", k=4),
                                       ACT.Copy).then_inc(hi_ok, 1)

                split_high(0)
                for c in range(KD):
                    act.wait_ge(w_at[c % RAW], 16 * (c // RAW + 1))
                    act.activation(hi[:, c, :], raw[:, c % RAW, :], ACT.Copy).then_inc(w_hi, 1)
                for t in range(1, TT):
                    split_high(t)

            @block.gpsimd
            def _(pool):
                for c in range(0, KD, 2):
                    split_weight(pool, c)

            @block.vector
            def _(dve):
                def split_low(t):
                    for h in range(2):
                        dve.wait_ge(hi_ok, 2 * t + h + 1)
                        dve.tensor_tensor(xT_lo[:, 4 * h:4 * h + 4, t * P:t * P + P], flip[:, (2 * t + h) % 4, :].rearrange("p (k n) -> p k n", k=4),
                                          plain(xT_hi[:, 4 * h:4 * h + 4, t * P:t * P + P]), ALU.subtract).then_inc(lo_ok, 1)

                split_low(0)
                for c in range(1, KD, 2):
                    split_weight(dve, c)
                split_low(1)
                for t in range(TT):
                    for h in range(2):
                        n = 2 * t + h
                        dve.wait_ge(made, n + 1)
                        dve.tensor_copy(acc[:, t, h * HALF:h * HALF + HALF], prod[:, n % 4, :]).then_inc(taken, 1)
                    if t + 2 < TT:
                        split_low(t + 2)

            @block.tensor
            def _(pe):
                def turn(t):
                    for h in range(2):
                        if t >= 2:
                            pe.wait_ge(lo_ok, 2 * (t - 2) + h + 1)
                        for c in range(4):
                            kk = 4 * h + c
                            last = pe.transpose(flip[:, (2 * t + h) % 4, c * P:c * P + P], acc[:, t, kk * P:kk * P + P], ident[:, :])
                        last.then_inc(flipped, 1)

                turn(0)
                turn(1)
                for t in range(TT):
                    pe.wait_ge(lo_ok, 2 * t + 2)
                    for h in range(2):
                        n = 2 * t + h
                        if n >= 4:
                            pe.wait_ge(taken, n - 3)
                        for c in range(KD):
                            if n == 0:
                                pe.wait_ge(w_lo[c % 2], c // 2 + 1)
                            last = split_product(pe, prod[:, n % 4, :], xT_hi[:, c, t * P:t * P + P], xT_lo[:, c, t * P:t * P + P],
                                                 hi[:, c, h * HALF:h * HALF + HALF], lo[:, c, h * HALF:h * HALF + HALF], c == 0, c == KD - 1)
                        last.then_inc(made, 1)
                    if t + 2 < TT:
                        turn(t + 2)


def layer(nc, x_prompt, x_sample, cache_ckv, cache_krope, cache_fk, cache_fv, cache_logf, g1_pre, g1_post, w1_gu, w1_down,
          gm_pre, gm_post, w_in, b_forget, g_q, w_q_up, g_kv, w_kv_up, w_out, g2_pre, g2_post, w2_gu, w2_down,
          identity, masks, triangle, pick, select, cos_sin, y, ckv_out, krope_out, fox_rows, logf_out):
    h1 = nc.dram_tensor("h1", [T, D], F32, kind="Internal").ap()
    h2 = nc.dram_tensor("h2", [T, D], F32, kind="Internal").ap()

    def x_rows(t):
        return x_prompt[t * P:t * P + P, :] if t < PT else x_sample

    def tile_of(a):
        return lambda t: a[t * P:t * P + P, :]

    with Tools(nc, "all") as k:
        ident = k.sb("ident", [P, P])
        ident_bf = k.sb("ident_bf", [P, P], BF16)
        mask_bf = k.sb("mask_bf", [P, 2 * P + NEW], BF16)
        consts_in = k.sem("consts_in")
        with Tools(nc, "consts") as c:
            wide = c.sb("wide", [P, 2 * P + NEW])
            with c.block() as block:
                @block.sync
                def _(sp):
                    sp.dma_start(ident[:, :], identity).then_inc(consts_in, 16)
                    sp.dma_start(wide[:, :], masks).then_inc(consts_in, 16)

                @block.vector
                def _(dve):
                    dve.wait_ge(consts_in, 32)
                    dve.tensor_copy(ident_bf[:, :], ident[:, :])
                    dve.tensor_copy(mask_bf[:, :], wide[:, :])

        acc = k.sb("acc", [P, TT, D])
        xT_at = nc.sbuf_base
        xT_hi, xT_lo = k.sb("xT_hi", [P, KD, T], F32R), k.sb("xT_lo", [P, KD, T], F32R)

        def spare(tag):
            return Region(nc, tag, xT_at, 2 * KD * T * 4)

        feed_forward(nc, "ffn1", ident, acc, xT_hi, xT_lo, w1_gu, w1_down, x_rows, None, g1_pre, (g1_post, 0.5, x_rows, tile_of(h1)), gm_pre)

        with Tools(nc, "mix") as m:
            logf, krope = m.sb("logf", [P, TT, H]), m.sb("krope", [P, TT, ROPE])
            with Tools(nc, "lat") as l:
                cq, ckv, gate = l.sb("cq", [P, TT, QL]), l.sb("ckv", [P, TT, KVL + ROPE]), l.sb("gate", [P, TT, H])
                input_projection(nc, "inp", w_in, xT_hi, xT_lo, fox_rows, cq, ckv, gate)
                up = spare("up_rows")
                kv_rows, q_rows = up.take("kv_rows", [P, PT, D]), up.take("q_rows", [P, TT, H * QW])
                ckvT_hi = up.take("ckvT_hi", [P, KC, T], F32R)
                with Tools(nc, "latT") as g:
                    cqT_hi, cqT_lo = g.sb("cqT_hi", [P, QC, T], F32R), g.sb("cqT_lo", [P, QC, T], F32R)
                    ckvT_lo = g.sb("ckvT_lo", [P, KC, T], F32R)
                    latent_norms(nc, "norms", ident, cq, ckv, gate, g_q, g_kv, b_forget, cos_sin, cqT_hi, cqT_lo, ckvT_hi, ckvT_lo,
                                 krope, logf, ckv_out, krope_out, logf_out)
                    q_raw = cq[:, :, :].rearrange("p t n -> p (t n)")[:, 0:QC * H * QW].rearrange("p (k n) -> p k n", k=QC)
                    kv_raw = ckv[:, :, :].rearrange("p t n -> p (t n)")[:, 0:KC * D].rearrange("p (k n) -> p k n", k=KC)
                    latent_up(nc, "up", w_q_up, w_kv_up, cos_sin, cqT_hi, cqT_lo, ckvT_hi, ckvT_lo, q_rows, kv_rows, q_raw, kv_raw)
            mla_prompt(nc, ident, ident_bf, mask_bf[:, 0:P], q_rows, kv_rows, krope, acc)
            with Tools(nc, "dec_all") as d:
                q_sample = d.sb("q_sample", [P, H * QW])
                with d.block() as block:
                    @block.vector
                    def _(dve):
                        dve.tensor_copy(q_sample[:, :], q_rows[:, PT, :])
                free = spare("dec_x")
                s = {name: free.take(name, shape) for name, shape in dict(
                    w_kv=[P, KC, D], qbd=[P, 4, DECB, P], qcT=[P, KC, DECB, H, NEW], aug_l=[P, DECB, P], knT=[P, 4, P], cnT=[P, KC, P], krnT=[ROPE, P],
                    qrT=[ROPE, DECB, H, NEW], aug_r=[P, KEYS], l_new=[P, NEW], fv0=[P, CK, FW], fv1=[P, CK, FW]).items()}
                head_pick = d.sb("head_pick", [P, H])
                pick_in = d.sem("pick_in")
                with d.block() as block:
                    @block.sync
                    def _(sp):
                        sp.dma_start(head_pick[:, :], pick).then_inc(pick_in, 16)
                        sp.wait_ge(pick_in, 16)
                sample_setup(nc, ident, q_sample, w_kv_up, select, cache_logf, fox_rows, ckv_out, krope_out, logf_out, s)
                sample_attention(nc, ident, ident_bf, mask_bf[:, 2 * P:2 * P + NEW], head_pick[:, :], s, cache_ckv, cache_krope, cache_fk, cache_fv, fox_rows, ckv_out, acc)
            with Tools(nc, "sums") as d:
                tri, ones = d.sb("tri", [P, P]), d.sb("ones", [P, P])
                free = spare("fox_x")
                rows = [free.take(f"rows{n}", [P, PT, FW]) for n in range(3)]
                tri_in = d.sem("tri_in")
                with d.block() as block:
                    @block.sync
                    def _(sp):
                        sp.dma_start(tri[:, :], triangle).then_inc(tri_in, 16)
                        sp.wait_ge(tri_in, 16)

                    @block.gpsimd
                    def _(pool):
                        pool.memset(ones[:, :], 1.0)
                fox_prompt(nc, ident, ident_bf, mask_bf[:, P:2 * P], tri, ones, logf, fox_rows, rows, acc)
            output_projection(nc, "outp", ident, w_out, xT_hi, xT_lo, acc)

        feed_forward(nc, "ffn2", ident, acc, xT_hi, xT_lo, w2_gu, w2_down, None, (gm_post, 1.0, tile_of(h1), tile_of(h2)), g2_pre,
                     (g2_post, 0.5, tile_of(h2), tile_of(y)), None)


def kernel(**inputs):
    import numpy as _np
    import concourse.bacc as _bacc
    from concourse import mybir as _mybir
    from concourse.bass_utils import run_bass_kernel_spmd as _run

    f32 = _np.float32
    shapes = dict(
        x_prompt=(SEQ, D), x_sample=(P, D), cache_mla_ckv=(DECB, PAST, KVL), cache_mla_krope=(DECB, PAST, ROPE), cache_fox_k=(DECB, PAST, FW),
        cache_fox_v=(DECB, PAST, FW), cache_fox_logf=(DECB, PAST, H), g_ffn1_pre=(D,), g_ffn1_post=(D,), w_ffn1_gu=(D, 2 * FF), w_ffn1_down=(FF, D),
        g_mix_pre=(D,), g_mix_post=(D,), w_in=(D, IN_COLS), b_forget=(H,), g_q_latent=(QL,), w_q_up=(QL, H * QW), g_kv_latent=(KVL,), w_kv_up=(KVL, D),
        w_out=(D, D), g_ffn2_pre=(D,), g_ffn2_post=(D,), w_ffn2_gu=(D, 2 * FF), w_ffn2_down=(FF, D))
    arrays = {n: _np.ascontiguousarray(inputs[n]).reshape(s) for n, s in shapes.items()}
    tile = _np.arange(P)
    hide = f32(-1e30)
    masks = _np.zeros((P, 2 * P + NEW), f32)
    masks[:, 0:P][tile[None, :] // 64 > tile[:, None] // 64] = hide
    masks[:, P:2 * P][tile[None, :] > tile[:, None]] = hide
    masks[:, 2 * P:][_np.arange(NEW)[None, :] > tile[:, None] % NEW] = hide
    select = _np.zeros((BH, DECB, P), f32)
    for b in range(DECB):
        for h in range(H):
            select[b * H + h, b, h * NEW:h * NEW + NEW] = 1
    pos = _np.concatenate([_np.arange(SEQ), _np.tile(PAST + _np.arange(NEW), DECB)]).astype(f32)
    freqs = f32(10000.0) ** (-_np.arange(ROPE // 2, dtype=f32) / f32(ROPE // 2))
    angle = pos[:, None] * freqs[None, :].astype(f32)
    cos_sin = _np.stack([_np.cos(angle), _np.sin(angle)], 1).astype(f32).reshape(TT, P, 2, ROPE // 2).transpose(1, 0, 2, 3)
    arrays |= dict(identity=_np.eye(P, dtype=f32), masks=masks, triangle=_np.triu(_np.ones((P, P), f32)),
                   pick=(tile[:, None] // NEW == _np.arange(H)[None, :]).astype(f32), select=select, cos_sin=_np.ascontiguousarray(cos_sin))
    outs = dict(y=(T, D), ckv=(T, KVL), krope=(T, ROPE), fox=(3, T, FW), logf=(T, H))

    nc = _bacc.Bacc("TRN2", target_bir_lowering=False, num_devices=1)
    args = [nc.dram_tensor(f"in_{n}", a.shape, _mybir.dt.from_np(a.dtype), kind="ExternalInput").ap() for n, a in arrays.items()]
    args += [nc.dram_tensor(f"out_{n}", s, _mybir.dt.float32, kind="ExternalOutput").ap() for n, s in outs.items()]
    layer(nc, *args)
    r = _run(nc, [{f"in_{n}": a for n, a in arrays.items()}], core_ids=[0]).results[0]
    y, ckv, krope, fox, logf = (r[f"out_{n}"] for n in outs)
    results = [y[:SEQ].reshape(1, SEQ, D), y[SEQ:].reshape(DECB, DECT, D)]
    for rows, lead in ((slice(0, SEQ), (1, 1, SEQ)), (slice(SEQ, T), (1, DECB, DECT))):
        results += [ckv[rows].reshape(*lead, KVL), krope[rows].reshape(*lead, ROPE), fox[1, rows].reshape(*lead, H, 64), fox[2, rows].reshape(*lead, H, 64),
                    logf[rows].reshape(*lead, H)]
    return tuple(results)
```

```python
import numpy as np
import concourse.bass as bass
from concourse import mybir
from contextlib import ExitStack

F32, F32R, BF16 = mybir.dt.float32, mybir.dt.float32r, mybir.dt.bfloat16
ACT, ALU, AX = mybir.ActivationFunctionType, mybir.AluOpType, mybir.AxisListType

P = 128
D = 1024
KD = D // P
SEQ, DECB, DECT, PAST = 1024, 8, 16, 512
T = SEQ + DECB * DECT
TT = T // P
PT = SEQ // P
TG, GN = 3, T // 3
FF = 2816
FC = FF // P
FB = 2
NB = FC // FB
EPS = 1e-6
HALF = 512


class Tools:

    def __init__(self, nc, tag):
        self.nc, self.tag, self.ctx, self.sems = nc, tag, ExitStack(), []

    def __enter__(self):
        return self

    def __exit__(self, *e):
        if self.sems and e[0] is None:
            with self.nc.Block() as block:
                @block.gpsimd
                def _(pool):
                    for s in self.sems:
                        pool.sem_clear(s)
        return self.ctx.__exit__(*e)

    def sb(self, name, shape, dt=F32):
        return self.ctx.enter_context(self.nc.sbuf_tensor(f"{self.tag}_{name}", shape, dt))

    def ps(self, name, shape, dt=F32):
        return self.ctx.enter_context(self.nc.psum_tensor(f"{self.tag}_{name}", shape, dt))

    def sem(self, name):
        self.sems.append(self.ctx.enter_context(self.nc.semaphore(f"{self.tag}_{name}")))
        return self.sems[-1]

    def block(self):
        return self.nc.Block()


def plain(ap):
    return ap.bitcast(F32)


def split_product(pe, out, w_hi, w_lo, x_hi, x_lo, first, last):
    pe.matmul(out, w_hi, x_hi, start=first, stop=False)
    pe.matmul(out, w_hi, x_lo, start=False, stop=False)
    return pe.matmul(out, w_lo, x_hi, start=False, stop=last)


class Region:

    def __init__(self, nc, tag, start, size):
        self.nc, self.tag, self.at, self.end = nc, tag, start, start + size

    def take(self, name, shape, dt=F32):
        size = int(np.prod(shape[1:])) * 4
        assert self.at + size <= self.end
        part = self.nc.alloc_sbuf_tensor_at(f"{self.tag}_{name}", shape, dt, offset=self.at)
        self.at += size
        return part


class Boundary:

    def __init__(self, k, name, acc, acc_ready, ident, xT_hi, xT_lo, post, pre, buffers, flips):
        self.acc, self.acc_ready, self.ident, self.xT_hi, self.xT_lo = acc, acc_ready, ident, xT_hi, xT_lo
        self.post, self.pre, self.flips = post, pre, flips
        self.gain, self.resid, self.normed_rows, self.junk = [
            [buffers[i].take(f"{name}_{what}{m}", [P, D])[:, :] for m in range(2)] for i, what in enumerate(("gain", "resid", "normed", "junk"))]
        self.lag = 2 if post else 0
        self.steps = TT + (self.lag + 2 if pre else 0)
        stats = k.sb(f"{name}_stats", [P, 4, 2, TT])
        self.ssq, self.mean, self.root, self.rstd = [stats[:, n, :, :] for n in range(4)]
        self.gain_in = [k.sem(f"{name}_gain_in{m}") for m in range(2)]
        if pre is None:
            self.resid, self.normed_rows = self.resid + self.normed_rows, None
        self.ring = len(self.resid)
        self.resid_in = [k.sem(f"{name}_resid_in{m}") for m in range(self.ring)]
        self.squared, self.mean_ok, self.root_ok, self.rstd_ok, self.normed = [
            [k.sem(f"{name}_{n}_{m}") for m in ("post", "pre")] for n in ("squared", "mean_ok", "root_ok", "rstd_ok", "normed")]
        self.by_dve = 0 if pre is not None else 2
        self.summed, self.stored, self.flipped, self.hi_ok, self.lo_ok = [k.sem(f"{name}_{n}") for n in ("summed", "stored", "flipped", "hi_ok", "lo_ok")]

    def stages(self, s):
        return [(m, t) for m, t, on in ((0, s, self.post), (1, s - self.lag, self.pre)) if on and 0 <= t < TT]

    def load_first(self, sp):
        if self.post:
            sp.dma_start(self.gain[0], self.post[0].partition_broadcast(P)).then_inc(self.gain_in[0], 16)
            for t in range(self.ring):
                sp.dma_start(self.resid[t], self.post[2](t)).then_inc(self.resid_in[t], 16)
        if self.pre is not None:
            sp.dma_start(self.gain[1], self.pre.partition_broadcast(P)).then_inc(self.gain_in[1], 16)

    def load_and_store(self, sp, end=TT, start=0):
        for t in range(start, end):
            sp.wait_ge(self.summed, t + 1)
            sp.dma_start(self.post[3](t), self.acc[:, t, :]).then_inc(self.stored, 16)
            if t + self.ring < TT:
                sp.dma_start(self.resid[t % self.ring], self.post[2](t + self.ring)).then_inc(self.resid_in[t % self.ring], 16)
        if end == TT:
            sp.wait_ge(self.stored, 16 * TT)

    def act(self, act, s):
        for m, t in self.stages(s):
            if m == 1 and self.post:
                act.wait_ge(self.summed, t + 1)
            else:
                self.acc_ready(act, t)
            if t:
                act.wait_ge(self.squared[m], t)
            act.activation(self.junk[m], self.acc[:, t, :], ACT.Square, accum_out=self.ssq[:, m, t:t + 1]).then_inc(self.squared[m], 1)
        for m, t in self.stages(s):
            act.wait_ge(self.mean_ok[m], t + 1)
            act.activation(self.root[:, m, t:t + 1], self.mean[:, m, t:t + 1], ACT.Sqrt).then_inc(self.root_ok[m], 1)
        t = s - self.lag - 1
        if self.pre is not None and 0 <= t < TT:
            for h in range(2):
                act.wait_ge(self.flipped, 2 * t + h + 1)
                act.activation(self.xT_hi[:, 4 * h:4 * h + 4, t * P:t * P + P], self.flips[(2 * t + h) % 4].rearrange("p (k n) -> p k n", k=4),
                               ACT.Copy).then_inc(self.hi_ok, 1)

    def dve(self, dve, s):
        for m, t in self.stages(s):
            factor = 1.0 if m else self.post[1]
            dve.wait_ge(self.squared[m], t + 1)
            dve.tensor_scalar(self.mean[:, m, t:t + 1], self.ssq[:, m, t:t + 1], 1.0 / (D * factor ** 2), EPS / factor ** 2, ALU.mult, ALU.add).then_inc(self.mean_ok[m], 1)
        t = s - self.lag - 2
        if self.pre is not None and 0 <= t < TT:
            for h in range(2):
                cols = slice(t * P, t * P + P)
                dve.wait_ge(self.hi_ok, 2 * t + h + 1)
                dve.tensor_tensor(self.xT_lo[:, 4 * h:4 * h + 4, cols], self.flips[(2 * t + h) % 4].rearrange("p (k n) -> p k n", k=4),
                                  plain(self.xT_hi[:, 4 * h:4 * h + 4, cols]), ALU.subtract).then_inc(self.lo_ok, 1)
        for m, t in self.stages(s):
            dve.wait_ge(self.root_ok[m], t + 1)
            dve.reciprocal(self.rstd[:, m, t:t + 1], self.root[:, m, t:t + 1]).then_inc(self.rstd_ok[m], 1)
        for m, t in self.stages(s):
            if t == 0:
                dve.wait_ge(self.gain_in[m], 16)
            if m and t >= 2:
                dve.wait_ge(self.flipped, 2 * (t - 2) + 2)
            dve.wait_ge(self.rstd_ok[m], t + 1)
            dst = self.normed_rows[t % 2] if m else self.acc[:, t, :]
            dve.scalar_tensor_tensor(dst, self.acc[:, t, :], self.rstd[:, m, t:t + 1], self.gain[m], ALU.mult, ALU.mult).then_inc(self.normed[m], 1)
        if s == TT - 1:
            for t in range(TT - self.by_dve, TT):
                self.add(dve, t)

    def add(self, eng, t):
        eng.wait_ge(self.normed[0], t + 1)
        eng.wait_ge(self.resid_in[t % self.ring], 16 * (t // self.ring + 1))
        if t == TT - self.by_dve:
            eng.wait_ge(self.summed, t)
        eng.tensor_tensor(self.acc[:, t, :], self.acc[:, t, :], self.resid[t % self.ring], ALU.add).then_inc(self.summed, 1)

    def pool(self, pool, t):
        if t < TT - self.by_dve:
            self.add(pool, t)

    def pe(self, pe, t):
        pe.wait_ge(self.normed[1], t + 1)
        for h in range(2):
            if t >= 2:
                pe.wait_ge(self.lo_ok, 2 * (t - 2) + h + 1)
            for c in range(4):
                kk = 4 * h + c
                last = pe.transpose(self.flips[(2 * t + h) % 4][:, c * P:c * P + P], self.normed_rows[t % 2][:, kk * P:kk * P + P], self.ident[:, :])
            last.then_inc(self.flipped, 1)


def gate_up_source(w_gu):
    return w_gu.rearrange("(k p) (s f n) -> p k s f n", p=P, s=2, n=P)


def load_gate_up(sp, raw, w_gu, at, loaded):
    for s in range(2):
        sp.dma_start(raw[:, :, s * P:s * P + P], gate_up_source(w_gu)[:, :, s, at, :].rearrange("p k f n -> p (k f) n")).then_inc(loaded, 16)


def feed_forward(nc, tag, ident, acc, xT_hi, xT_lo, w_gu, w_down, gu_raw, gu_in, rows_of, entry_pre, exit_post, exit_pre, load_next):
    with Tools(nc, tag) as k:
        starts = {}

        def buffer(name, shape, dt=F32):
            starts[name] = nc.sbuf_base
            return k.sb(name, shape, dt)

        def borrowed(*names):
            return [Region(nc, tag, starts[name], 2 * D * 4) for name in names]

        for j in range(FB):
            buffer(f"gu_raw{j}", [P, KD, 2 * P])
        gu_hi = [buffer(f"gu_hi{j}", [P, KD, 2 * P], F32R) for j in range(FB)]
        gu_lo = [buffer(f"gu_lo{j}", [P, KD, 2 * P], F32R) for j in range(FB)]
        dn_raw = buffer("dn_raw", [P, FB, D])
        dn_hi = buffer("dn_hi", [P, FB, D], F32R)
        dn_lo = buffer("dn_lo", [P, FB, D], F32R)
        a_hi = buffer("a_hi", [P, FB, T], F32R)
        a_lo = buffer("a_lo", [P, FB, T], F32R)
        silu = k.sb("silu", [P, 2, GN])
        prod = k.sb("prod", [P, 2, GN])
        gate_ps = k.ps("gate_ps", [P, 2, HALF])
        up_ps = k.ps("up_ps", [P, 2, HALF])
        DR = 3
        down_ps = k.ps("down_ps", [P, DR + 1, HALF])
        dn_in = k.sem("dn_in")
        hi_ok = k.sem("hi_ok")
        W = FB + 1
        lo_ok = k.sem("lo_ok")
        GU = FB * TG
        gu_ready = k.sem("gu_ready")
        silu_ok = k.sem("silu_ok")
        prod_ok = k.sem("prod_ok")
        a_hi_ok = k.sem("a_hi_ok")
        a_lo_ok = k.sem("a_lo_ok")
        DU = TT * 2
        down_ready = k.sem("down_ready")
        added = k.sem("added")
        bit_hi, bit_lo = k.sem("bit_hi"), k.sem("bit_lo")
        row_in = [k.sem(f"row_in{t}") for t in range(TT if rows_of else 0)]
        dn_src = w_down.rearrange("(f p) n -> p f n", p=P)
        LAST = NB - 1

        def row_there(act, t):
            if rows_of:
                act.wait_ge(row_in[t], 16)

        def row_summed(act, t):
            act.wait_ge(added, LAST * DU + (DR + 2 * t + 2))

        entry = Boundary(k, "entry", acc, row_there, ident, xT_hi, xT_lo, None, entry_pre,
                         borrowed("dn_hi", "dn_lo", "a_hi", "a_lo"),
                         [down_ps[:, n, :] for n in range(4)]) if rows_of else None
        leave = Boundary(k, "exit", acc, row_summed, ident, xT_hi, xT_lo, exit_post, exit_pre,
                         borrowed("gu_raw0", "gu_raw1", "gu_hi0", "gu_hi1"),
                         [gate_ps[:, 0, :], gate_ps[:, 1, :], up_ps[:, 0, :], up_ps[:, 1, :]])

        with k.block() as block:
            @block.sync
            def _(sp):
                def gate_up(i, ahead, j):
                    sp.wait_ge(lo_ok, i * W + (ahead * W + j + 1))
                    load_gate_up(sp, gu_raw[j], w_gu, bass.ds(i * FB + (ahead * FB + j), 1), gu_in[j])

                def down(i, ahead):
                    sp.wait_ge(lo_ok, i * W + (ahead * W + W))
                    sp.dma_start(dn_raw[:, :, :], dn_src[:, bass.ds(i * FB + ahead * FB, FB), :]).then_inc(dn_in, 16)

                if rows_of:
                    for t in range(TT):
                        sp.dma_start(acc[:, t, :], rows_of(t)).then_inc(row_in[t], 16)
                        if t == 0:
                            entry.load_first(sp)
                        if t in (2, TT - 1):
                            gate_up(0, 0, t // (TT - 1))
                down(0, 0)
                with sp.Fori(0, LAST) as i:
                    for j in range(FB):
                        gate_up(i, 1, j)
                    down(i, 1)
                sp.wait_ge(gu_ready, LAST * GU + (2 * GU))
                leave.load_first(sp)
                load_next(sp)
                leave.load_and_store(sp)

            @block.gpsimd
            def _(pool):
                def gate_up(i, ahead, j):
                    pool.wait_ge(hi_ok, i * W + (ahead * W + j + 1))
                    pool.tensor_tensor(gu_lo[j][:, :, :], gu_raw[j][:, :, :], plain(gu_hi[j][:, :, :]), ALU.subtract).then_inc(lo_ok, 1)

                def down(i):
                    pool.wait_ge(hi_ok, i * W + W)
                    pool.tensor_tensor(dn_lo[:, :, :], dn_raw[:, :, :], plain(dn_hi[:, :, :]), ALU.subtract).then_inc(lo_ok, 1)

                pool.sem_inc(lo_ok, W)
                if not rows_of:
                    pool.wait_ge(lo_ok, W + 1)
                for j in range(0 if rows_of else 1, FB):
                    gate_up(0, 0, j)
                with pool.Fori(0, LAST) as i:
                    down(i)
                    for j in range(FB):
                        gate_up(i, 1, j)
                down(LAST)
                for s in range(TT):
                    leave.pool(pool, s)

            @block.scalar
            def _(act):
                def gate_up(i, ahead, j):
                    act.wait_ge(gu_in[j], i * 32 + (ahead * 32 + 32))
                    act.wait_ge(gu_ready, i * GU + (ahead * GU + TG * (j + 1)))
                    act.activation(gu_hi[j][:, :, :], gu_raw[j][:, :, :], ACT.Copy).then_inc(hi_ok, 1)

                def units(i):
                    for j in range(FB):
                        for g in range(TG):
                            u = j * TG + g
                            act.wait_ge(gu_ready, i * GU + (GU + u + 1))
                            act.activation(silu[:, u % 2, :], gate_ps[:, u % 2, 0:GN], ACT.Silu).then_inc(silu_ok, 1)
                            act.wait_ge(prod_ok, i * GU + (2 + u + 1))
                            act.activation(a_hi[:, j, g * GN:g * GN + GN], prod[:, u % 2, :], ACT.Copy).then_inc(a_hi_ok, 1)
                        if j == 0:
                            act.wait_ge(dn_in, i * 16 + 16)
                            act.wait_ge(down_ready, i * DU + 1)
                            act.activation(dn_hi[:, :, :], dn_raw[:, :, :], ACT.Copy).then_inc(hi_ok, 1)

                for s in range(entry.steps if entry else 0):
                    entry.act(act, s)
                    if s in (2, 6):
                        gate_up(0, 0, s // 6)
                if not entry:
                    act.wait_ge(gu_in[0], 32)
                    for kk in range(KD):
                        act.activation(gu_hi[0][:, kk, :], gu_raw[0][:, kk, :], ACT.Copy).then_inc(bit_hi if kk < KD - 1 else hi_ok, 1)
                    gate_up(0, 0, 1)
                with act.Fori(0, LAST) as i:
                    units(i)
                    for j in range(FB):
                        gate_up(i, 1, j)
                units(LAST)
                for s in range(leave.steps):
                    leave.act(act, s)

            @block.vector
            def _(dve):
                def units(i):
                    for j in range(FB):
                        for g in range(TG):
                            u = j * TG + g
                            dve.wait_ge(silu_ok, i * GU + (u + 1))
                            dve.tensor_tensor(prod[:, u % 2, :], up_ps[:, u % 2, 0:GN], silu[:, u % 2, :], ALU.mult).then_inc(prod_ok, 1)
                            dve.wait_ge(a_hi_ok, i * GU + (u + 1))
                            dve.tensor_tensor(a_lo[:, j, g * GN:g * GN + GN], prod[:, u % 2, :], plain(a_hi[:, j, g * GN:g * GN + GN]),
                                              ALU.subtract).then_inc(a_lo_ok, 1)

                def down(i, t, first=False):
                    for h in range(2):
                        m = 2 * t + h
                        dst = acc[:, t, h * HALF:h * HALF + HALF]
                        dve.wait_ge(down_ready, i * DU + (1 + m + 1))
                        if first:
                            dve.tensor_copy(dst, down_ps[:, m % DR, :]).then_inc(added, 1)
                        else:
                            dve.tensor_tensor(dst, down_ps[:, m % DR, :], dst, ALU.add).then_inc(added, 1)

                dve.sem_inc(prod_ok, 2)
                dve.sem_inc(added, DR)
                for s in range(entry.steps if entry else 0):
                    entry.dve(dve, s)
                for kk in range(0 if entry else KD):
                    dve.wait_ge(bit_hi, kk + 1) if kk < KD - 1 else dve.wait_ge(hi_ok, 1)
                    dve.tensor_tensor(gu_lo[0][:, kk, :], gu_raw[0][:, kk, :], plain(gu_hi[0][:, kk, :]), ALU.subtract).then_inc(bit_lo if kk < KD - 1 else lo_ok, 1)
                units(0)
                for t in range(TT):
                    down(0, t, True)
                with dve.Fori(1, LAST) as i:
                    units(i)
                    for t in range(TT):
                        down(i, t)
                units(LAST)
                for s in range(leave.steps + 1):
                    if s < TT:
                        down(LAST, s)
                    if s:
                        leave.dve(dve, s - 1)

            @block.tensor
            def _(pe):
                def gate_up(i, j, g, between=lambda s: None):
                    u = j * TG + g
                    bits = not rows_of and isinstance(i, int) and (i, j, g) == (0, 0, 0)
                    if g == 0 and not bits:
                        pe.wait_ge(lo_ok, i * W + (W + j + 1))
                    pe.wait_ge(prod_ok, i * GU + (u + 1))
                    toks = slice(g * GN, g * GN + GN)
                    for s, bank in enumerate((gate_ps, up_ps)):
                        for kk in range(KD):
                            if bits and s == 0:
                                pe.wait_ge(bit_lo, kk + 1) if kk < KD - 1 else pe.wait_ge(lo_ok, W + 1)
                            last = split_product(pe, bank[:, u % 2, 0:GN], gu_hi[j][:, kk, s * P:s * P + P], gu_lo[j][:, kk, s * P:s * P + P],
                                                 xT_hi[:, kk, toks], xT_lo[:, kk, toks], kk == 0, kk == KD - 1)
                        if s == 1:
                            last.then_inc(gu_ready, 1)
                        between(s)

                def down(i, t):
                    if t == 0:
                        pe.wait_ge(lo_ok, i * W + (W + W))
                    pe.wait_ge(a_lo_ok, i * GU + ((FB - 1) * TG + t * P // GN + 1))
                    for h in range(2):
                        m = 2 * t + h
                        pe.wait_ge(added, i * DU + (m + 1))
                        for j in range(FB):
                            last = split_product(pe, down_ps[:, m % DR, :], a_hi[:, j, t * P:t * P + P], a_lo[:, j, t * P:t * P + P],
                                                 dn_hi[:, j, h * HALF:h * HALF + HALF], dn_lo[:, j, h * HALF:h * HALF + HALF], j == 0, j == FB - 1)
                        last.then_inc(down_ready, 1)

                def block_products(i, first=False):
                    for j in range(FB):
                        for g in range(TG):
                            if first and entry and j == 0:
                                size = TT // TG
                                for t in range(g * size + (2 if g else 0), (g + 1) * size):
                                    entry.pe(pe, t)
                                pe.wait_ge(entry.lo_ok, 2 * (g + 1) * size)
                                gate_up(i, j, g, lambda s: entry.pe(pe, (g + 1) * size + s) if g + 1 < TG else None)
                            else:
                                gate_up(i, j, g)

                pe.sem_inc(gu_ready, GU)
                pe.sem_inc(down_ready, 1)
                block_products(0, True)
                for t in range(TT):
                    down(0, t)
                with pe.Fori(1, LAST) as i:
                    block_products(i)
                    for t in range(TT):
                        down(i, t)
                block_products(LAST)
                AFTER = 4
                for t in range(TT + AFTER):
                    if t < TT:
                        down(LAST, t)
                    if leave.pre is not None and t >= AFTER:
                        leave.pe(pe, t - AFTER)


QL, KVL, ROPE, NOPE, VD = 384, 256, 32, 64, 64
H = 8
FW = H * 64
QW = NOPE + ROPE
IN_COLS = QL + KVL + ROPE + 3 * FW + H
FOX_AT = QL + KVL + ROPE
GATE_AT = IN_COLS - H
QC, KC = QL // P, KVL // P
KH = KD // 2


def load_in_group(sp, raw, w_in, columns, loaded):
    src = w_in.rearrange("(k p) n -> p k n", p=P)
    for h in range(2):
        at = 0
        for c0, w in columns:
            sp.dma_start(raw[h][:, :, at:at + w], src[:, h * KH:h * KH + KH, c0:c0 + w]).then_inc(loaded[h], 16)
            at += w


def input_projection(nc, tag, w_in, raw, raw_at, first_in, xT_hi, xT_lo, fox_rows, cq, ckv, gate):
    cols = [[(FOX_AT + n * FW, FW)] for n in range(3)] + [[(0, QL), (GATE_AT, H)], [(QL, KVL + ROPE)]]
    width = [sum(w for _, w in c) for c in cols]
    NG = len(cols)
    R = 3
    with Tools(nc, tag) as k:
        stage = k.sb("stage", [P, R, HALF])
        k.sb("before_raw", [P, (raw_at - nc.sbuf_base) // 4])
        assert nc.sbuf_base == raw_at
        k.sb("raw_place", [P, 2 * KH * HALF])
        hi = [k.sb(f"hi{h}", [P, KH, HALF], F32R) for h in range(2)]
        lo = [k.sb(f"lo{h}", [P, KH, HALF], F32R) for h in range(2)]
        prod = k.ps("prod", [P, R, HALF])
        w_at = [first_in] + [[k.sem(f"w_at{n}{h}") for h in range(2)] for n in range(1, NG)]
        hi_ok = k.sem("hi_ok")
        lo_ok = k.sem("lo_ok")
        piece_used = k.sem("piece_used")
        tile_ok = k.sem("tile_ok")
        taken = k.sem("taken")
        stored = [k.sem(f"stored{s}") for s in range(R)]

        with k.block() as block:
            @block.sync
            def _(sp):
                for n in range(NG):
                    if n + 1 < NG:
                        sp.wait_ge(lo_ok, KD * n + KD)
                        load_in_group(sp, raw, w_in, cols[n + 1], w_at[n + 1])
                    if n < 3:
                        for t in range(TT):
                            sp.wait_ge(taken, R + n * TT + t + 1)
                            sp.dma_start(fox_rows[n, t * P:t * P + P, :], stage[:, t % R, :]).then_inc(stored[t % R], 16)
                for s in range(R):
                    sp.wait_ge(stored[s], 3 * TT // R * 16)

            @block.scalar
            def _(act):
                for n in range(NG):
                    for c in range(KD):
                        h, kk = divmod(c, KH)
                        if kk == 0:
                            act.wait_ge(w_at[n][h], 16 * len(cols[n]))
                        if n:
                            act.wait_ge(piece_used, (n - 1) * (KD - 1) + c + 1) if c < KD - 1 else act.wait_ge(tile_ok, n * TT)
                        act.activation(hi[h][:, kk, 0:width[n]], raw[h][:, kk, 0:width[n]], ACT.Copy).then_inc(hi_ok, 1)

            @block.vector
            def _(dve):
                def split_low(n):
                    for c in range(KD):
                        h, kk = divmod(c, KH)
                        dve.wait_ge(hi_ok, n * KD + c + 1)
                        dve.tensor_tensor(lo[h][:, kk, 0:width[n]], raw[h][:, kk, 0:width[n]], plain(hi[h][:, kk, 0:width[n]]), ALU.subtract).then_inc(lo_ok, 1)

                dve.sem_inc(taken, R)
                split_low(0)
                for n in range(NG):
                    for t in range(TT):
                        if t == TT - 1 and n + 1 < NG:
                            split_low(n + 1)
                        dve.wait_ge(tile_ok, n * TT + t + 1)
                        if n < 3:
                            if n or t >= R:
                                dve.wait_ge(stored[t % R], 16 * (n * TT // R + t // R))
                            dve.tensor_copy(stage[:, t % R, :], prod[:, t % R, :]).then_inc(taken, 1)
                        elif n == 3:
                            dve.tensor_copy(gate[:, t, :], prod[:, t % R, QL:QL + H])
                            dve.tensor_copy(cq[:, t, :], prod[:, t % R, 0:QL]).then_inc(taken, 1)
                        else:
                            dve.tensor_copy(ckv[:, t, :], prod[:, t % R, 0:KVL + ROPE]).then_inc(taken, 1)

            @block.tensor
            def _(pe):
                def group(n, w):
                    for t in range(TT):
                        pe.wait_ge(taken, n * TT + (t + 1))
                        for c in range(KD):
                            h, kk = divmod(c, KH)
                            if t == 0:
                                pe.wait_ge(lo_ok, n * KD + (c + 1))
                            last = split_product(pe, prod[:, t % R, 0:w], xT_hi[:, c, t * P:t * P + P], xT_lo[:, c, t * P:t * P + P],
                                                 hi[h][:, kk, 0:w], lo[h][:, kk, 0:w], c == 0, c == KD - 1)
                            if t == TT - 1 and c < KD - 1:
                                last.then_inc(piece_used, 1)
                        last.then_inc(tile_ok, 1)

                with pe.Fori(0, 3) as n:
                    group(n, HALF)
                for n in range(3, NG):
                    group(n, width[n])


def latents(nc, tag, ident, cq, ckv, gate, g_q, g_kv, b_forget, w_q_up, w_kv_up, cos_sin, q_rows, kv_rows, region, krope, logf, ckv_out, krope_out, logf_out):
    R = 3
    HQ = H * QW // 2
    with Tools(nc, tag) as k:
        gq_bc, gkv_bc, bf_bc = k.sb("gq_bc", [P, QL]), k.sb("gkv_bc", [P, KVL]), k.sb("bf_bc", [P, H])
        cs = k.sb("cs", [P, TT, 2, ROPE // 2])
        ssq, mean, root, rstd = [k.sb(n, [P, TT, 2]) for n in ("ssq", "mean", "root", "rstd")]
        z, mag, e, lnp = [k.sb(n, [P, TT, H]) for n in ("z", "mag", "e", "lnp")]
        rot_k = k.sb("rot_k", [P, TT, 4, ROPE // 2])
        rot = k.sb("rot", [P, 4, H, ROPE // 2])
        q_raw, kv_raw = k.sb("q_raw", [P, QC, H * QW]), k.sb("kv_raw", [P, KC, D])
        q_hi, q_lo = k.sb("q_hi", [P, QC, H * QW], F32R), k.sb("q_lo", [P, QC, H * QW], F32R)
        kv_hi, kv_lo = k.sb("kv_hi", [P, KC, D], F32R), k.sb("kv_lo", [P, KC, D], F32R)
        cqT_hi, cqT_lo = region.take("cqT_hi", [P, R, QC, P], F32R), region.take("cqT_lo", [P, R, QC, P], F32R)
        junk = region.take("junk", [P, QL + KVL])
        ckvT_hi, ckvT_lo = k.sb("ckvT_hi", [P, R, KC, P], F32R), k.sb("ckvT_lo", [P, R, KC, P], F32R)
        flip = k.ps("flip", [P, 4, HALF])
        prod = k.ps("prod", [P, 4, HALF])
        w_at = [k.sem(f"w_at{n}") for n in range(2)]
        consts_in, w_hi, w_q_lo, w_kv_lo, squared, mean_ok, root_ok, rstd_ok, normed, flipped, hi_ok, lo_ok, made, taken, rotated, roped = [
            k.sem(n) for n in ("consts_in", "w_hi", "w_q_lo", "w_kv_lo", "squared", "mean_ok", "root_ok", "rstd_ok", "normed", "flipped", "hi_ok", "lo_ok",
                               "made", "taken", "rotated", "roped")]
        zed, magged, exped, lned, gated, key_rotated, key_roped, stored = [
            k.sem(n) for n in ("zed", "magged", "exped", "lned", "gated", "key_rotated", "key_roped", "stored")]
        x1, x2 = ckv[:, :, KVL:KVL + ROPE // 2], ckv[:, :, KVL + ROPE // 2:KVL + ROPE]
        both = ((cq, QL, cqT_hi, cqT_lo, QC), (ckv, KVL, ckvT_hi, ckvT_lo, KC))

        def made_by(t):
            return 2 * (t + 1) + 2 * min(t + 1, PT)

        with k.block() as block:
            @block.sync
            def _(sp):
                sp.dma_start(gq_bc[:, :], g_q.partition_broadcast(P)).then_inc(consts_in, 16)
                sp.dma_start(gkv_bc[:, :], g_kv.partition_broadcast(P)).then_inc(consts_in, 16)
                sp.dma_start(bf_bc[:, :], b_forget.partition_broadcast(P)).then_inc(consts_in, 16)
                sp.dma_start(cs[:, :, :, :], cos_sin).then_inc(consts_in, 16)
                sp.dma_start(q_raw[:, :, :], w_q_up.rearrange("(k p) n -> p k n", p=P)).then_inc(w_at[0], 16)
                sp.dma_start(kv_raw[:, :, :], w_kv_up.rearrange("(k p) n -> p k n", p=P)).then_inc(w_at[1], 16)
                sp.wait_ge(key_roped, 2)
                sp.dma_start(krope_out.rearrange("(t p) n -> p t n", p=P), krope[:, :, :]).then_inc(stored, 16)
                sp.wait_ge(gated, 1)
                sp.dma_start(logf_out.rearrange("(t p) n -> p t n", p=P), logf[:, :, :]).then_inc(stored, 16)
                sp.wait_ge(normed, 2 * TT)
                sp.dma_start(ckv_out.rearrange("(t p) n -> p t n", p=P), ckv[:, :, 0:KVL]).then_inc(stored, 16)
                sp.wait_ge(stored, 48)

            @block.gpsimd
            def _(pool):
                pool.wait_ge(w_hi, 1)
                pool.tensor_tensor(q_lo[:, :, :], q_raw[:, :, :], plain(q_hi[:, :, :]), ALU.subtract).then_inc(w_q_lo, 1)

            @block.scalar
            def _(act):
                def evacuate(t):
                    for h in range(2):
                        n = made_by(t - 1) + h
                        act.wait_ge(made, n + 1)
                        act.activation(q_rows[:, t, h * HQ:h * HQ + HQ], prod[:, n % 4, 0:HQ], ACT.Copy).then_inc(taken, 1)
                    for h in range(2 if t < PT else 0):
                        n = made_by(t - 1) + 2 + h
                        act.wait_ge(made, n + 1)
                        act.activation(kv_rows[:, t, h * HALF:h * HALF + HALF], prod[:, n % 4, :], ACT.Copy).then_inc(taken, 1)

                def split_high(t):
                    for m, (_, _, hi, _, pieces) in enumerate(both):
                        act.wait_ge(flipped, 2 * t + m + 1)
                        if t >= R:
                            act.wait_ge(made, made_by(t - R))
                        act.activation(hi[:, t % R, :, :], flip[:, (2 * t + m) % 4, 0:pieces * P].rearrange("p (k n) -> p k n", n=P), ACT.Copy).then_inc(hi_ok, 1)

                for t in range(TT + 2):
                    if t < TT:
                        if t:
                            act.wait_ge(squared, 2 * t)
                        for m, (rows, w, _, _, _) in enumerate(both):
                            act.activation(junk[:, m * QL:m * QL + w], rows[:, t, 0:w], ACT.Square, accum_out=ssq[:, t, m:m + 1]).then_inc(squared, 1)
                        act.wait_ge(mean_ok, 2 * t + 2)
                        act.activation(root[:, t, :], mean[:, t, :], ACT.Sqrt).then_inc(root_ok, 1)
                    for n, (raw, hi) in enumerate(((q_raw, q_hi), (kv_raw, kv_hi))):
                        if t == n:
                            act.wait_ge(w_at[n], 16)
                            act.activation(hi[:, :, :], raw[:, :, :], ACT.Copy).then_inc(w_hi, 1)
                    if 0 <= t - 1 < TT:
                        split_high(t - 1)
                    if t >= 2:
                        evacuate(t - 2)
                    if t == 5:
                        act.wait_ge(zed, 1)
                        act.activation(mag[:, :, :], z[:, :, :], ACT.Abs).then_inc(magged, 1)
                        act.wait_ge(magged, 1)
                        act.activation(e[:, :, :], mag[:, :, :], ACT.Exp, scale=-1.0).then_inc(exped, 1)
                        act.wait_ge(exped, 1)
                        act.activation(lnp[:, :, :], e[:, :, :], ACT.Ln, bias=1.0).then_inc(lned, 1)

            @block.vector
            def _(dve):
                def split_low(t):
                    for m, (_, _, hi, lo, pieces) in enumerate(both):
                        dve.wait_ge(hi_ok, 2 * t + m + 1)
                        dve.tensor_tensor(lo[:, t % R, :, :], flip[:, (2 * t + m) % 4, 0:pieces * P].rearrange("p (k n) -> p k n", n=P),
                                          plain(hi[:, t % R, :, :]), ALU.subtract).then_inc(lo_ok, 1)

                def rope(t):
                    dve.wait_ge(taken, made_by(t - 1) + 2)
                    heads = q_rows[:, t, :].rearrange("p (h n) -> p h n", n=QW)
                    q1, q2 = heads[:, :, NOPE:NOPE + ROPE // 2], heads[:, :, NOPE + ROPE // 2:QW]
                    c = cs[:, t, 0, :].unsqueeze(1).broadcast_to([P, H, ROPE // 2])
                    s = cs[:, t, 1, :].unsqueeze(1).broadcast_to([P, H, ROPE // 2])
                    if t:
                        dve.wait_ge(roped, 2 * t)
                    for n, (x, y) in enumerate(((q1, c), (q2, s), (q1, s), (q2, c))):
                        last = dve.tensor_tensor(rot[:, n, :, :], x, y, ALU.mult)
                    last.then_inc(rotated, 1)
                    dve.wait_ge(rotated, t + 1)
                    dve.tensor_tensor(q1, rot[:, 0, :, :], rot[:, 1, :, :], ALU.subtract).then_inc(roped, 1)
                    dve.tensor_tensor(q2, rot[:, 2, :, :], rot[:, 3, :, :], ALU.add).then_inc(roped, 1)

                for t in range(TT + 2):
                    if t < TT:
                        dve.wait_ge(squared, 2 * t + 2)
                        for m, (_, w, _, _, _) in enumerate(both):
                            dve.tensor_scalar(mean[:, t, m:m + 1], ssq[:, t, m:m + 1], 1.0 / w, EPS, ALU.mult, ALU.add).then_inc(mean_ok, 1)
                        if t == 0:
                            dve.wait_ge(consts_in, 64)
                        dve.wait_ge(root_ok, t + 1)
                        dve.reciprocal(rstd[:, t, :], root[:, t, :]).then_inc(rstd_ok, 1)
                        dve.wait_ge(rstd_ok, t + 1)
                        for m, (rows, w, _, _, _) in enumerate(both):
                            gain = (gq_bc, gkv_bc)[m]
                            dve.scalar_tensor_tensor(rows[:, t, 0:w], rows[:, t, 0:w], rstd[:, t, m:m + 1], gain[:, :], ALU.mult, ALU.mult).then_inc(normed, 1)
                    if t == 1:
                        dve.wait_ge(w_hi, 2)
                        dve.tensor_tensor(kv_lo[:, :, :], kv_raw[:, :, :], plain(kv_hi[:, :, :]), ALU.subtract).then_inc(w_kv_lo, 1)
                    if 0 <= t - 1 < TT:
                        split_low(t - 1)
                    if t == 2:
                        c, s = cs[:, :, 0, :], cs[:, :, 1, :]
                        dve.tensor_tensor(rot_k[:, :, 0, :], x1, c, ALU.mult)
                        dve.tensor_tensor(rot_k[:, :, 1, :], x2, s, ALU.mult)
                        dve.tensor_tensor(rot_k[:, :, 2, :], x1, s, ALU.mult)
                        dve.tensor_tensor(rot_k[:, :, 3, :], x2, c, ALU.mult).then_inc(key_rotated, 1)
                        dve.wait_ge(key_rotated, 1)
                        dve.tensor_tensor(krope[:, :, 0:ROPE // 2], rot_k[:, :, 0, :], rot_k[:, :, 1, :], ALU.subtract).then_inc(key_roped, 1)
                        dve.tensor_tensor(krope[:, :, ROPE // 2:ROPE], rot_k[:, :, 2, :], rot_k[:, :, 3, :], ALU.add).then_inc(key_roped, 1)
                        dve.tensor_tensor(z[:, :, :], gate[:, :, :], bf_bc[:, :].unsqueeze(1).broadcast_to([P, TT, H]), ALU.add).then_inc(zed, 1)
                    if t == 7:
                        dve.wait_ge(lned, 1)
                        dve.scalar_tensor_tensor(logf[:, :, :], z[:, :, :], 0.0, lnp[:, :, :], ALU.min, ALU.subtract).then_inc(gated, 1)
                    if t >= 2:
                        rope(t - 2)

            @block.tensor
            def _(pe):
                def turn(t):
                    for m, (rows, _, _, _, pieces) in enumerate(both):
                        pe.wait_ge(normed, 2 * t + m + 1)
                        if t >= 2:
                            pe.wait_ge(lo_ok, 2 * (t - 2) + m + 1)
                        for c in range(pieces):
                            last = pe.transpose(flip[:, (2 * t + m) % 4, c * P:c * P + P], rows[:, t, c * P:c * P + P], ident[:, :])
                        last.then_inc(flipped, 1)

                def up(t, m, w_hi_, w_lo_, width):
                    _, _, hi, lo, pieces = both[m]
                    pe.wait_ge(lo_ok, 2 * t + m + 1)
                    for h in range(2):
                        n = made_by(t - 1) + 2 * m + h
                        if n >= 4:
                            pe.wait_ge(taken, n - 3)
                        for c in range(pieces):
                            last = split_product(pe, prod[:, n % 4, 0:width], hi[:, t % R, c, :], lo[:, t % R, c, :],
                                                 w_hi_[:, c, h * width:h * width + width], w_lo_[:, c, h * width:h * width + width], c == 0, c == pieces - 1)
                        last.then_inc(made, 1)

                turn(0)
                for t in range(TT):
                    if t + 1 < TT:
                        turn(t + 1)
                    if t == 0:
                        pe.wait_ge(w_q_lo, 1)
                    up(t, 0, q_hi, q_lo, HQ)
                    if t == 0:
                        pe.wait_ge(w_kv_lo, 1)
                    if t < PT:
                        up(t, 1, kv_hi, kv_lo, HALF)


PAIRS = H // 2
NM = 32 * 3
KROWS = NM + PT
HALVES = SEQ // HALF
HT = HALF // P
CHUNKS = [(h, t, max(h * HALF, t * P)) for h in range(HALVES) for t in range((h + 1) * HT)]
NCH = len(CHUNKS)
LAST_OF_HALF = [max(n for n, c in enumerate(CHUNKS) if c[0] == h) for h in range(HALVES)]
PREP_AT = {0: (0, 1), 1: (2, 3)}
MAX_AT = {2: (0, 1), 3: (2, 3), 4: (4,), 5: (5,), 6: (6,), 7: (7,)}
ROWS_AT = {8: 0, 9: 1}
PREP = 4
PASS = PREP // 2 + 1
assert NCH % 2 == 0 and KROWS <= P and HALVES == 2


def prompt_attention(nc, tag, ident, ident_bf, mask_bf, kdim, scale, loaded, load_count, stage_head, q_ops, stage_ops, v_of, o_rows, o_at, load_next):
    with Tools(nc, tag) as k:
        q_st = [k.sb(f"q_st{b}", [P, PT, kdim]) for b in range(2)]
        k_st = [k.sb(f"k_st{b}", [P, PT, kdim]) for b in range(2)]
        v_st = [k.sb(f"v_st{b}", [P, PT, VD + 1]) for b in range(2)]
        qT_hi = [k.sb(f"qT_hi{b}", [KROWS, SEQ], F32R) for b in range(2)]
        qT_lo = [k.sb(f"qT_lo{b}", [KROWS, SEQ], F32R) for b in range(2)]
        kT_hi = [k.sb(f"kT_hi{b}", [KROWS, SEQ], F32R) for b in range(2)]
        kT_lo = [k.sb(f"kT_lo{b}", [KROWS, SEQ], F32R) for b in range(2)]
        nmax = [k.sb(f"nmax{b}", [P, PT, PT]) for b in range(2)]
        probs = k.sb("probs", [P, 2, HALF])
        inverse = k.sb("inverse", [P, 2, HALVES, HT])
        rough = k.ps("rough", [P, SEQ])
        turn = k.ps("turn", [P, 2, HALF])
        scores = k.ps("scores", [P, 2, HALF])
        out = k.ps("out", [P, HALVES, HT, P])
        cleared = k.sem("cleared")
        rows_cleared = k.sem("rows_cleared")
        maxima_hi = k.sem("maxima_hi")
        staged = k.sem("staged")
        v_staged = k.sem("v_staged")
        prepared = k.sem("prepared")
        prep_hi = k.sem("prep_hi")
        turn_out = [k.sem(f"turn_out{n}") for n in range(2)]
        rough_ready = k.sem("rough_ready")
        max_ok = k.sem("max_ok")
        rows_ready = k.sem("rows_ready")
        s_ready = k.sem("s_ready")
        exp_ok = k.sem("exp_ok")
        pv_ok = k.sem("pv_ok")
        inverse_ok = k.sem("inverse_ok")
        o_taken = k.sem("o_taken")
        CLEARS = 2 * 2

        def prep_parts(b, r):
            st, hi, lo = (q_st, qT_hi, qT_lo) if r % 2 == 0 else (k_st, kT_hi, kT_lo)
            cols = slice(r // 2 * HALF, r // 2 * HALF + HALF)
            return st[b], hi[b][0:kdim, cols], lo[b][0:kdim, cols]

        with k.block() as block:
            @block.sync
            def _(sp):
                load_next(sp)

            @block.gpsimd
            def _(pool):
                for b in range(2):
                    pool.memset(nmax[b][:, :, :], 0.0).then_inc(cleared, 1)
                    pool.memset(v_st[b][:, :, VD:VD + 1], 1.0).then_inc(cleared, 1)
                if load_count:
                    pool.wait_ge(loaded, load_count * 16)
                with pool.Fori(0, PAIRS) as i:
                    for b in range(2):
                        pool.wait_ge(prepared, i * (2 * PREP) + (b + 1) * PREP)
                        stage_head(pool, i * 2 + b, q_st[b], k_st[b], staged)
                        pool.wait_ge(pv_ok, i * (2 * NCH) + (b + 1) * NCH)
                        pool.tensor_copy(v_st[b][:, :, 0:VD], v_of(i * 2 + b)).then_inc(v_staged, 1)

            @block.scalar
            def _(act):
                def exponent(n, b, s):
                    _, _, c0 = CHUNKS[s]
                    w = HALF - c0 % HALF
                    act.wait_ge(s_ready, n * NCH + (s + 1))
                    act.activation(probs[:, s % 2, 0:w], scores[:, s % 2, 0:w], ACT.Exp).then_inc(exp_ok, 1)

                def preparation(n, b, step):
                    for r in PREP_AT.get(step, ()):
                        _, hi, _ = prep_parts(b, r)
                        act.wait_ge(prepared, n * PREP + (2 * PREP + r + 1))
                        act.activation(hi, turn[0:kdim, r % 2, :], ACT.Copy, scale=scale if r % 2 == 0 else 1.0).then_inc(prep_hi, 1)
                    if step in ROWS_AT:
                        g = ROWS_AT[step]
                        act.wait_ge(rows_ready, n * HALVES + (g + 1))
                        act.activation(qT_hi[b][NM:KROWS, g * HALF:g * HALF + HALF], turn[0:PT, g % 2, :], ACT.Copy).then_inc(maxima_hi, 1)

                def head(n, b, follows):
                    for s in range(NCH):
                        if s + 1 < NCH:
                            exponent(n, b, s + 1)
                        elif follows:
                            exponent(n + 1, 1 - b, 0)
                        if follows:
                            preparation(n + 1, 1 - b, s)

                act.wait_ge(rows_cleared, 4)
                for step in range(NCH):
                    preparation(0, 0, step)
                act.wait_ge(rows_cleared, 8)
                exponent(0, 0, 0)
                with act.Fori(0, PAIRS - 1) as i:
                    for b in range(2):
                        head(i * 2 + b, b, True)
                for b in range(2):
                    head(H - 2 + b, b, b == 0)

            @block.vector
            def _(dve):
                def preparation(n, b, step):
                    for r in PREP_AT.get(step, ()):
                        _, hi, lo = prep_parts(b, r)
                        dve.wait_ge(prep_hi, n * PREP + (r + 1))
                        dve.scalar_tensor_tensor(lo, turn[0:kdim, r % 2, :], scale if r % 2 == 0 else 1.0, plain(hi), ALU.mult, ALU.subtract).then_inc(turn_out[r % 2], 1)
                    for t in MAX_AT.get(step, ()):
                        at = t % 2 * HALF if t < HT else 0
                        dve.wait_ge(rough_ready, n * PT + (t + 1))
                        dve.tensor_reduce(nmax[b][:, t, t:t + 1], rough[:, at:at + (t + 1) * P], axis=AX.X, op=ALU.max, negate=True).then_inc(max_ok, 1)

                    if step in ROWS_AT:
                        g = ROWS_AT[step]
                        cols = slice(g * HALF, g * HALF + HALF)
                        dve.wait_ge(maxima_hi, n * HALVES + (g + 1))
                        dve.tensor_tensor(qT_lo[b][NM:KROWS, cols], turn[0:PT, g % 2, :], plain(qT_hi[b][NM:KROWS, cols]), ALU.subtract).then_inc(turn_out[g % 2], 1)

                def normalise(n, b, h):
                    dve.wait_ge(pv_ok, n * NCH + (2 * NCH + LAST_OF_HALF[h] + 1))
                    dve.reciprocal(inverse[:, b, h, :].unsqueeze(2), out[:, h, :, VD:VD + 1]).then_inc(inverse_ok, 1)
                    dve.wait_ge(inverse_ok, n * HALVES + (h + 1))
                    dve.tensor_tensor(o_rows[:, h * HT:h * HT + HT, bass.ds(n * VD + o_at, VD)], out[:, h, :, 0:VD],
                                      inverse[:, b, h, :].unsqueeze(2).broadcast_to([P, HT, VD]), ALU.mult).then_inc(o_taken, 1)

                def head(n, b, follows):
                    for s in range(NCH):
                        if follows:
                            preparation(n + 1, 1 - b, s)
                        for h in range(HALVES):
                            if s == min(LAST_OF_HALF[h] + 1, NCH - 1):
                                normalise(n, b, h)

                def clear(b):
                    for x in (qT_hi, qT_lo, kT_lo, kT_hi):
                        rows = slice(kdim // 32 * 32, KROWS)
                        if x is not kT_hi:
                            dve.memset(plain(x[b][rows, :]), 0.0).then_inc(rows_cleared, 1)
                        else:
                            if NM > rows.start:
                                dve.memset(plain(x[b][rows.start:NM, :]), 0.0)
                            dve.memset(plain(x[b][NM:KROWS, :]), 1.0).then_inc(rows_cleared, 1)

                clear(0)
                clear(1)
                dve.wait_ge(rows_cleared, 8)
                dve.wait_ge(cleared, CLEARS)
                for step in range(NCH):
                    preparation(0, 0, step)
                with dve.Fori(0, PAIRS - 1) as i:
                    for b in range(2):
                        head(i * 2 + b, b, True)
                for b in range(2):
                    head(H - 2 + b, b, b == 0)

            @block.tensor
            def _(pe):
                pe.sem_inc(prepared, 2 * PREP)
                pe.sem_inc(exp_ok, 2)
                pe.sem_inc(pv_ok, 2 * NCH)
                for free in (*turn_out, max_ok):
                    pe.sem_inc(free, 1)
                pe.sem_inc(o_taken, HALVES)

                def preparation(n, b, step):
                    for r in PREP_AT.get(step, ()):
                        st, _, _ = prep_parts(b, r)
                        if r < 2:
                            pe.wait_ge(staged, n * stage_ops + (stage_ops if r else q_ops))
                        pe.wait_ge(turn_out[r % 2], n * PASS + (r // 2 + 1))
                        for c in range(HT):
                            last = pe.transpose(turn[0:kdim, r % 2, c * P:c * P + P], st[:, r // 2 * HT + c, :], ident[:, :])
                        last.then_inc(prepared, 1)
                    for t in MAX_AT.get(step, ()):
                        if t == 0:
                            for bank in range(2):
                                pe.wait_ge(turn_out[bank], n * PASS + (1 + PREP // 2))
                        pe.wait_ge(max_ok, n * PT + (1 + (0 if t < 2 else t - 1 if t < HT else t)))
                        at = t % 2 * HALF if t < HT else 0
                        cols = (t + 1) * P
                        for c0 in range(0, cols, HALF):
                            w = min(HALF, cols - c0)
                            diagonal = c0 + w == cols
                            last = pe.matmul(rough[:, at + c0:at + c0 + w], qT_hi[b][0:kdim, t * P:t * P + P], kT_hi[b][0:kdim, c0:c0 + w], start=True, stop=not diagonal)
                            if diagonal:
                                last = pe.matmul(rough[:, at + cols - P:at + cols], ident_bf[:, :], mask_bf, start=False, stop=True)
                        last.then_inc(rough_ready, 1)
                    if step in ROWS_AT:
                        g = ROWS_AT[step]
                        pe.wait_ge(turn_out[g % 2], n * PASS + PASS)
                        pe.wait_ge(max_ok, n * PT + (1 + (g + 1) * HT))
                        for c in range(HT):
                            last = pe.transpose(turn[0:PT, g % 2, c * P:c * P + P], nmax[b][:, g * HT + c, :], ident[:, :])
                        last.then_inc(rows_ready, 1)

                def score(n, b, s):
                    h, t, c0 = CHUNKS[s]
                    w = (h + 1) * HALF - c0
                    if s == 0 or h != CHUNKS[s - 1][0]:
                        pe.wait_ge(turn_out[h % 2], n * PASS + (1 + PASS))
                    pe.wait_ge(exp_ok, n * NCH + (s + 1))
                    diagonal = c0 == t * P
                    last = split_product(pe, scores[:, s % 2, 0:w], kT_hi[b][:, t * P:t * P + P], kT_lo[b][:, t * P:t * P + P],
                                         qT_hi[b][:, c0:c0 + w], qT_lo[b][:, c0:c0 + w], True, not diagonal)
                    if diagonal:
                        last = pe.matmul(scores[:, s % 2, 0:P], mask_bf, ident_bf[:, :], start=False, stop=True)
                    last.then_inc(s_ready, 1)

                def head(n, b, follows):
                    for s, (h, t, c0) in enumerate(CHUNKS):
                        if s + 1 < NCH:
                            score(n, b, s + 1)
                        elif follows:
                            score(n + 1, 1 - b, 0)
                        if follows:
                            preparation(n + 1, 1 - b, s)
                        pe.wait_ge(exp_ok, n * NCH + (2 + s + 1))
                        if t == 0:
                            pe.wait_ge(o_taken, n * HALVES + (h + 1))
                        if s == 0:
                            pe.wait_ge(v_staged, n + 1)
                        for u in range(c0 // P, (h + 1) * HT):
                            last = pe.matmul(out[:, h, u % HT, 0:VD + 1], probs[:, s % 2, u * P - c0:u * P - c0 + P], v_st[b][:, t, :], start=(t == 0 and u == c0 // P), stop=(s in LAST_OF_HALF))
                        last.then_inc(pv_ok, 1)

                pe.wait_ge(cleared, CLEARS)
                pe.wait_ge(rows_cleared, 4)
                for step in range(NCH):
                    preparation(0, 0, step)
                score(0, 0, 0)
                pe.wait_ge(rows_cleared, 8)
                with pe.Fori(0, PAIRS - 1) as i:
                    for b in range(2):
                        head(i * 2 + b, b, True)
                for b in range(2):
                    head(H - 2 + b, b, b == 0)


def mla_prompt(nc, ident, ident_bf, mask_bf, q_rows, kv_rows, krope, o_rows, load_next):
    def stage(pool, n, q_st, k_st, done):
        pool.tensor_copy(q_st[:, :, :], q_rows[:, 0:PT, bass.ds(n * QW, QW)]).then_inc(done, 1)
        pool.tensor_copy(k_st[:, :, 0:NOPE], kv_rows[:, :, bass.ds(n * (NOPE + VD), NOPE)]).then_inc(done, 1)
        pool.tensor_copy(k_st[:, :, NOPE:QW], krope[:, 0:PT, :]).then_inc(done, 1)

    def v_of(n):
        return kv_rows[:, :, bass.ds(n * (NOPE + VD) + NOPE, VD)]

    prompt_attention(nc, "mla", ident, ident_bf, mask_bf, QW, QW ** -0.5, None, 0, stage, 1, 3, v_of, o_rows, 0, load_next)


def load_fox_rows(sp, fox_rows, rows, loaded):
    for n in range(3):
        sp.dma_start(rows[n][:, :, :], fox_rows[n, 0:SEQ, :].rearrange("(t p) n -> p t n", p=P)).then_inc(loaded, 16)


def fox_prompt(nc, ident, ident_bf, mask_bf, tri, ones, logf, rows, loaded, o_rows, load_next):
    scale = 64 ** -0.5
    with Tools(nc, "decay") as k:
        q_decay = k.sb("q_decay", [P, PT, H, 2])
        k_decay = k.sb("k_decay", [P, PT, H, 2])
        with Tools(nc, "cumsum") as c:
            within = c.ps("within", [P, PT, H])
            totals = c.ps("totals", [P, PT, H])
            cum = c.sb("cum", [P, PT, H])
            cum_hi = c.sb("cum_hi", [P, PT, H], F32R)
            cum_lo = c.sb("cum_lo", [P, PT, H])
            before = c.sb("before", [P, PT, H])
            summed, step = c.sem("summed"), c.sem("step")
            with k.block() as block:
                @block.tensor
                def _(pe):
                    every = logf[:, 0:PT, :]
                    pe.matmul(within[:, :, :], tri, every, start=True, stop=True)
                    pe.matmul(totals[:, :, :], ones, every, start=True, stop=True).then_inc(summed, 1)

                @block.vector
                def _(dve):
                    dve.memset(before[:, 0, :], 0.0).then_inc(step, 1)
                    dve.wait_ge(summed, 1)
                    for t in range(1, PT):
                        dve.wait_ge(step, t)
                        dve.tensor_tensor(before[:, t, :], before[:, t - 1, :], totals[:, t - 1, :], ALU.add).then_inc(step, 1)
                    dve.wait_ge(step, PT)
                    dve.tensor_tensor(cum[:, :, :], within[:, :, :], before[:, :, :], ALU.add).then_inc(step, 1)
                    dve.wait_ge(step, PT + 1)
                    dve.tensor_copy(cum_hi[:, :, :], cum[:, :, :]).then_inc(step, 1)
                    dve.wait_ge(step, PT + 2)
                    dve.tensor_tensor(cum_lo[:, :, :], cum[:, :, :], plain(cum_hi[:, :, :]), ALU.subtract).then_inc(step, 1)
                    dve.wait_ge(step, PT + 3)
                    for n, part in enumerate((plain(cum_hi[:, :, :]), cum_lo[:, :, :])):
                        dve.tensor_scalar(q_decay[:, :, :, n], part, 1 / scale, None, ALU.mult)
                        dve.tensor_scalar(k_decay[:, :, :, n], part, -1.0, None, ALU.mult)

        def stage(pool, n, q_st, k_st, done):
            pool.tensor_copy(q_st[:, :, 0:64], rows[0][:, :, bass.ds(n * 64, 64)]).then_inc(done, 1)
            pool.tensor_copy(q_st[:, :, 64:66].unsqueeze(2), q_decay[:, :, bass.ds(n, 1), :]).then_inc(done, 1)
            pool.memset(q_st[:, :, 66:68], 1 / scale).then_inc(done, 1)
            pool.tensor_copy(k_st[:, :, 0:64], rows[1][:, :, bass.ds(n * 64, 64)]).then_inc(done, 1)
            pool.memset(k_st[:, :, 64:66], 1.0).then_inc(done, 1)
            pool.tensor_copy(k_st[:, :, 66:68].unsqueeze(2), k_decay[:, :, bass.ds(n, 1), :]).then_inc(done, 1)

        def v_of(n):
            return rows[2][:, :, bass.ds(n * VD, VD)]

        prompt_attention(nc, "fox", ident, ident_bf, mask_bf, 68, scale, loaded, 3, stage, 3, 6, v_of, o_rows, H * VD, load_next)


NEW = DECT
CK = PAST // P
KEYS = PAST + NEW
BH = DECB * H
assert BH == 64 and H * NEW == P and PAST % 64 == 0 and NEW <= 64


def load_setup_rows(sp, cache_logf, fox_rows, ckv_out, krope_out, w_kv_up, logf_out, s, rows_in):
    tail = slice(SEQ, T)
    for dst, src in ((s["logs_in"][:, :, :, :], cache_logf.rearrange("b (p r) h -> p b r h", r=CK)), (s["fq"][:, :], fox_rows[0, tail, :]),
                     (s["fk"][:, :], fox_rows[1, tail, :]), (s["cn"][:, :], ckv_out[tail, :]), (s["kn"][:, :], krope_out[tail, :]),
                     (s["w_kv"][:, :, :], w_kv_up.rearrange("(k p) n -> p k n", p=P)),
                     (s["new_logs"][:, :, :], logf_out[tail, :].rearrange("(b t) h -> t b h", t=NEW))):
        sp.dma_start(dst, src).then_inc(rows_in, 16)


def load_keys(sp, at, kr, fk, cache_krope, cache_fk, loaded):
    for dst, src in ((kr, cache_krope), (fk, cache_fk)):
        sp.dma_start(dst[:, :, :], cache_rows(src, at)).then_inc(loaded, 16)


def cache_rows(src, at):
    return src[at, :, :].rearrange("b (p r) n -> p (b r) n", r=CK)


def sample_setup(nc, ident, q_sample, select, rows_in, load_first_keys, s):
    with Tools(nc, "setup") as k:
        logs_r = k.sb("logs_r", [P, CK, DECB, H])
        logs = k.sb("logs", [BH, KEYS])
        ones = k.sb("ones", [BH, KEYS])
        cum = k.sb("cum", [BH, KEYS])
        logs_in, new_logs, fq, fk, cn, kn = [s[n] for n in ("logs_in", "new_logs", "fq", "fk", "cn", "kn")]
        qnT = k.sb("qnT", [NOPE, H, P])
        wkT = k.sb("wkT", [NOPE, H, KVL])
        flip = k.ps("flip", [P, 4, HALF])
        regrouped, sel_at, flipped, moved, ready, scanned = [k.sem(n) for n in ("regrouped", "sel_at", "flipped", "moved", "ready", "scanned")]
        sel_low, sel_high = s["aug_l"][0:BH, :, :], s["aug_l"][BH:P, :, :]


        with k.block() as block:
            @block.sync
            def _(sp):
                sp.dma_start(sel_low, select).then_inc(sel_at, 16)
                sp.dma_start(sel_high, select).then_inc(sel_at, 16)
                load_first_keys(sp)
                sp.wait_ge(sel_at, 32)

            @block.gpsimd
            def _(pool):
                pool.memset(s["qbd"][:, :, :, :], 0.0).then_inc(ready, 1)
                pool.memset(ones[:, :], 1.0).then_inc(ready, 1)

            @block.tensor
            def _(pe):
                pe.wait_ge(rows_in, 112)
                pe.wait_ge(regrouped, 1)
                for r in range(CK):
                    last = pe.transpose(flip[0:BH, 0, r * P:r * P + P], logs_r[:, r, :, :].rearrange("p b h -> p (b h)"), ident[:, :])
                last.then_inc(flipped, 1)
                for n, rows in ((1, fq), (2, fk)):
                    for c in range(4):
                        last = pe.transpose(flip[:, n, c * P:c * P + P], rows[:, c * P:c * P + P], ident[:, :])
                    last.then_inc(flipped, 1)
                for c in range(KC):
                    pe.transpose(flip[:, 3, c * P:c * P + P], cn[:, c * P:c * P + P], ident[:, :])
                pe.transpose(flip[0:ROPE, 3, KVL:KVL + P], kn[:, :], ident[:, :])
                pe.transpose(flip[0:BH, 3, KVL + P:KVL + P + NEW], new_logs[:, :, :].rearrange("t b h -> t (b h)"), ident[0:NEW, 0:NEW]).then_inc(flipped, 1)
                heads = q_sample[:, :].rearrange("p (h n) -> p h n", n=QW)
                for n in range(4, 8):
                    pe.wait_ge(moved, n - 3)
                    for c in range(4):
                        h = (n % 2) * 4 + c
                        if n < 6:
                            last = pe.transpose(flip[0:NOPE, n % 4, c * P:c * P + P], heads[:, h, 0:NOPE], ident[:, :])
                        else:
                            last = pe.transpose(flip[0:ROPE, n % 4, c * P:c * P + P], heads[:, h, NOPE:QW], ident[:, :])
                    last.then_inc(flipped, 1)
                for n in range(8, 12):
                    pe.wait_ge(moved, n - 3)
                    for c in range(4):
                        h = (n - 8) * 2 + c // 2
                        last = pe.transpose(flip[0:NOPE, n % 4, c * P:c * P + P], s["w_kv"][:, c % 2, h * P:h * P + NOPE], ident[:, :])
                    last.then_inc(flipped, 1)
                for n in range(12, 16):
                    pe.wait_ge(moved, 12 if n == 12 else n - 3)
                    c = (n - 12) // 2
                    for i in range(4):
                        h = n % 2 * 4 + i
                        last = pe.matmul(flip[:, n % 4, i * P:i * P + P], wkT[:, h, c * P:c * P + P], qnT[:, h, :], start=True, stop=True)
                    last.then_inc(flipped, 1)

            @block.vector
            def _(dve):
                dve.wait_ge(rows_in, 112)
                dve.tensor_copy(logs_r[:, :, :, :].rearrange("p r b h -> p b r h"), logs_in[:, :, :, :]).then_inc(regrouped, 1)
                dve.wait_ge(flipped, 1)
                dve.tensor_copy(logs[:, 0:PAST].rearrange("q (p r) -> q r p", r=CK), flip[0:BH, 0, :].rearrange("q (r p) -> q r p", r=CK)).then_inc(moved, 1)
                dve.wait_ge(flipped, 2)
                dve.wait_ge(ready, 1)
                for j in range(2):
                    for c in range(4):
                        src = flip[64 * j:64 * j + 64, 1, c * P:c * P + P].rearrange("p (b t) -> p b t", t=NEW)
                        last = dve.tensor_scalar(s["qbd"][64 * j:64 * j + 64, c, :, (2 * c + j) * NEW:(2 * c + j + 1) * NEW], src, 64 ** -0.5, None, ALU.mult)
                last.then_inc(moved, 1)
                dve.wait_ge(flipped, 3)
                dve.tensor_copy(s["knT"][:, :, :], flip[:, 2, :].rearrange("p (c n) -> p c n", c=4)).then_inc(moved, 1)
                dve.wait_ge(flipped, 4)
                dve.tensor_copy(s["cnT"][:, :, :], flip[:, 3, 0:KVL].rearrange("p (c n) -> p c n", c=KC))
                dve.tensor_copy(s["krnT"][:, :], flip[0:ROPE, 3, KVL:KVL + P])
                dve.tensor_copy(logs[:, PAST:KEYS], flip[0:BH, 3, KVL + P:KVL + P + NEW]).then_inc(moved, 1)
                for n in range(4, 8):
                    dve.wait_ge(flipped, n + 1)
                    hs = slice(n % 2 * 4, n % 2 * 4 + 4)
                    if n < 6:
                        dve.tensor_copy(qnT[:, hs, :], flip[0:NOPE, n % 4, :].rearrange("p (h n) -> p h n", h=4)).then_inc(moved, 1)
                    else:
                        dve.tensor_copy(s["qrT"][:, :, hs, :].rearrange("p b h t -> p h b t"), flip[0:ROPE, n % 4, :].rearrange("p (h b t) -> p h b t", h=4, t=NEW)).then_inc(moved, 1)
                for n in range(8, 12):
                    dve.wait_ge(flipped, n + 1)
                    dve.tensor_copy(wkT[:, (n - 8) * 2:(n - 8) * 2 + 2, :], flip[0:NOPE, n % 4, :].rearrange("p (h n) -> p h n", h=2)).then_inc(moved, 1)
                for n in range(12, 16):
                    dve.wait_ge(flipped, n + 1)
                    c, hs = (n - 12) // 2, slice(n % 2 * 4, n % 2 * 4 + 4)
                    dve.tensor_copy(s["qcT"][:, c, :, hs, :].rearrange("p b h t -> p h b t"), flip[:, n % 4, :].rearrange("p (h b t) -> p h b t", h=4, t=NEW)).then_inc(moved, 1)
                dve.wait_ge(ready, 2)
                dve.wait_ge(moved, 16)
                dve.tensor_tensor_scan(cum[:, :], ones[:, :], logs[:, :], 0.0, ALU.mult, ALU.add).then_inc(scanned, 1)
                dve.wait_ge(scanned, 1)
                dve.tensor_scalar(s["aug_r"][0:BH, :], cum[:, :], -1.0, None, ALU.mult)
                dve.memset(s["aug_r"][BH:P, :], 1.0)
                dve.tensor_copy(s["l_new"][BH:P, :], cum[:, PAST:KEYS]).then_inc(scanned, 1)
                dve.wait_ge(scanned, 2)
                dve.wait_ge(sel_at, 32)
                grid = sel_high.rearrange("q b (h t) -> q (b h) t", t=NEW)
                dve.tensor_tensor(grid, grid, s["l_new"][BH:P, :].unsqueeze(1).broadcast_to([BH, BH, NEW]), ALU.mult)


def sample_attention(nc, ident, ident_bf, mask_bf, head_pick, s, cache_ckv, cache_krope, cache_fk, cache_fv, fox_rows, ckv_out, o_rows, prompt_rows, prompt_loaded, keys_in):
    with Tools(nc, "dec") as k:
        ckv_in, kr, fk = [[s[f"{n}{b}"] for b in range(2)] for n in ("ckv_in", "kr", "fk")]
        ckv = [k.sb(f"ckv{b}", [P, CK, KVL]) for b in range(2)]
        fv = [s["fv0"], s["fv1"]]
        cn = [k.sb(f"cn{b}", [NEW, KVL]) for b in range(2)]
        vn = [k.sb(f"vn{b}", [NEW, FW]) for b in range(2)]
        ckvT = k.sb("ckvT", [P, KC, PAST])
        krT = k.sb("krT", [ROPE, PAST])
        fkT = k.sb("fkT", [P, 4, PAST])
        qc = [k.sb(f"qc{b}", [P, KC, P]) for b in range(2)]
        qr = [k.sb(f"qr{b}", [ROPE, P]) for b in range(2)]
        qf = [k.sb(f"qf{b}", [P, 4, P]) for b in range(2)]
        qa = [k.sb(f"qa{b}", [P, P]) for b in range(2)]
        p_sb = [k.sb(f"p_sb{m}", [P, KEYS]) for m in range(2)]
        pT = [k.sb(f"pT{m}", [P, CK, P]) for m in range(2)]
        pTn = [k.sb(f"pTn{m}", [NEW, P]) for m in range(2)]
        nmax, total, inverse = [k.sb(n, [P, 2, 2]) for n in ("nmax", "total", "inverse")]
        picked = k.sb("picked", [P, H, 64])
        folded = k.sb("folded", [P, 64])
        o_mla = k.sb("o_mla", [P, DECB, KVL])
        o_fox = k.sb("o_fox", [P, DECB, 64])
        flip = k.ps("flip", [P, 2, HALF])
        scores = k.ps("scores", [P, 3 * HALF])
        mla_at, fox_at = 0, 3 * HALF - KEYS
        pT_ps = k.ps("pT_ps", [P, 2, HALF])
        o_ps = k.ps("o_ps", [P, HALF])
        out_bank = [pT_ps[:, 0, :], o_ps[:, :]]
        span = [scores[:, mla_at:mla_at + KEYS], scores[:, fox_at:fox_at + KEYS]]
        cached_part = [span[0][:, 0:PAST], span[1][:, NEW:KEYS]]
        new_part = [span[0][:, PAST:KEYS], span[1][:, 0:NEW]]
        p_cached = [p_sb[0][:, 0:PAST], p_sb[1][:, NEW:KEYS]]
        p_new = [p_sb[0][:, PAST:KEYS], p_sb[1][:, 0:NEW]]
        pTn_ps = [scores[0:NEW, HALF + (m + 1) * P:HALF + (m + 2) * P] for m in range(2)]
        values_in = [k.sem(f"values_in{b}") for b in range(2)]
        staged = k.sem("staged")
        kept = k.sem("kept")
        flip_ready = k.sem("flip_ready")
        flip_ok = [k.sem("flip_ok_act"), k.sem("flip_ok_dve")]
        s_ready = k.sem("s_ready")
        raw_max, max_ok, exp_ok, pt_ready, pt_ok = [k.sem(n) for n in ("raw_max", "max_ok", "exp_ok", "pt_ready", "pt_ok")]
        pv_ok = k.sem("pv_ok")
        inverse_ok, picked_ok, folded_ok, mla_taken, fox_taken = [k.sem(n) for n in ("inverse_ok", "picked_ok", "folded_ok", "mla_taken", "fox_taken")]
        LOADS, STAGES, FLIPS = 3, 4, 7
        flips = [([P, c, "ckv"], ckvT[:, c, :]) for c in range(KC)] + [([ROPE, 0, "kr"], krT[:, :])] + [([P, c, "fk"], fkT[:, c, :]) for c in range(4)]

        def flip_rows(b, g, r):
            (_, c, what), _ = flips[g]
            source = {"ckv": ckv_in, "kr": kr, "fk": fk}[what][b]
            return source[:, r, :] if what == "kr" else source[:, r, c * P:c * P + P]

        def flip_number(b, g):
            return b * FLIPS + g

        with k.block() as block:
            @block.sync
            def _(sp):
                def values(i, b):
                    sp.wait_ge(pv_ok, i * 4 + (2 * b + 2))
                    sp.dma_start(fv[b][:, :, :], cache_rows(cache_fv, bass.ds(i * 2 + b, 1))).then_inc(values_in[b], 16)
                    new = bass.ds(i * (2 * NEW) + (b * NEW + SEQ), NEW)
                    sp.dma_start(cn[b][:, :], ckv_out[new, :]).then_inc(values_in[b], 16)
                    sp.dma_start(vn[b][:, :], fox_rows[2, new, :]).then_inc(values_in[b], 16)

                with sp.Fori(0, DECB // 2 - 1) as i:
                    for b in range(2):
                        values(i, b)
                        sp.wait_ge(flip_ready, i * (2 * FLIPS) + (2 * FLIPS + (b + 1) * FLIPS))
                        load_keys(sp, bass.ds(i * 2 + (b + 2), 1), kr[b], fk[b], cache_krope, cache_fk, keys_in[b])
                        sp.wait_ge(kept, i * 2 + (b + 3))
                        sp.dma_start(ckv_in[b][:, :, :], cache_rows(cache_ckv, bass.ds(i * 2 + (b + 2), 1))).then_inc(keys_in[b], 16)
                for b in range(2):
                    values(DECB // 2 - 1, b)

            @block.gpsimd
            def _(pool):
                with pool.Fori(0, DECB // 2) as i:
                    for b in range(2):
                        n = i * 2 + b
                        pool.wait_ge(s_ready, i * 4 + (2 * b + 2))
                        pool.tensor_copy(qc[b][:, :, :].unsqueeze(2), s["qcT"][:, :, bass.ds(n, 1), :, :].rearrange("p c b h t -> p c b (h t)")).then_inc(staged, 1)
                        pool.tensor_copy(qr[b][:, :].unsqueeze(1), s["qrT"][:, bass.ds(n, 1), :, :].rearrange("p b h t -> p b (h t)")).then_inc(staged, 1)
                        pool.tensor_copy(qf[b][:, :, :].unsqueeze(2), s["qbd"][:, :, bass.ds(n, 1), :]).then_inc(staged, 1)
                        pool.tensor_copy(qa[b][:, :].unsqueeze(1), s["aug_l"][:, bass.ds(n, 1), :]).then_inc(staged, 1)

            def take_flips(eng, copy, parity, i2, b):
                for g, ((parts, _, _), dst) in enumerate(flips):
                    G = flip_number(b, g)
                    if G % 2 == parity:
                        eng.wait_ge(flip_ready, i2 * (2 * FLIPS) + (2 * FLIPS + G + 1))
                        copy(dst, flip[0:parts, parity, :]).then_inc(flip_ok[parity], 1)

            @block.scalar
            def _(act):
                def copy(dst, src):
                    return act.activation(dst, src, ACT.Copy)

                def keep(i2, b):
                    act.wait_ge(keys_in[b], i2 * (16 * LOADS) + 16 * LOADS)
                    act.wait_ge(pv_ok, i2 * 4 + (2 * b + 2))
                    copy(ckv[b][:, :, :], ckv_in[b][:, :, :]).then_inc(kept, 1)

                def exponents(i2, b):
                    act.wait_ge(max_ok, i2 * 4 + (2 * b + 2))
                    for m in range(2):
                        act.activation(p_sb[m][:, :], span[m], ACT.Exp, bias=nmax[:, b, m:m + 1],
                                       scale=QW ** -0.5 if m == 0 else 1.0, accum_out=total[:, b, m:m + 1]).then_inc(exp_ok, 1)

                def stream(i, b, follows):
                    def cached(m):
                        return copy(pT[m][:, :, :], pT_ps[:, m, :].rearrange("p (r n) -> p r n", r=CK))

                    act.wait_ge(pt_ready, i * 4 + (2 * b + 1))
                    cached(0)
                    act.wait_ge(pt_ready, i * 4 + (2 * b + 2))
                    copy(pTn[0][:, :], pTn_ps[0])
                    copy(pTn[1][:, :], pTn_ps[1]).then_inc(pt_ok, 1)
                    cached(1).then_inc(pt_ok, 1)
                    if follows:
                        take_flips(act, copy, 0, i + b, 1 - b)
                        keep(i + b, 1 - b)
                        exponents(i + b, 1 - b)

                take_flips(act, copy, 0, 0, 0)
                keep(0, 0)
                exponents(0, 0)
                with act.Fori(0, DECB // 2 - 1) as i:
                    for b in range(2):
                        stream(i, b, True)
                for b in range(2):
                    stream(DECB // 2 - 1, b, b == 0)

            @block.vector
            def _(dve):
                def maxima(i2, b):
                    for m in range(2):
                        dve.wait_ge(s_ready, i2 * 4 + (4 + 2 * b + m + 1))
                        dve.tensor_reduce(nmax[:, b, m:m + 1], span[m], axis=AX.X, op=ALU.max, negate=True).then_inc(max_ok if m else raw_max, 1)
                        if m == 0:
                            dve.wait_ge(raw_max, i2 * 2 + (b + 1))
                            dve.tensor_scalar(nmax[:, b, 0:1], nmax[:, b, 0:1], QW ** -0.5, None, ALU.mult).then_inc(max_ok, 1)

                def outputs(i, b):
                    n, n2 = i * 2 + b, i * 4 + 2 * b
                    dve.wait_ge(exp_ok, n2 + 2)
                    dve.reciprocal(inverse[:, b, :], total[:, b, :]).then_inc(inverse_ok, 1)
                    dve.wait_ge(inverse_ok, n + 1)
                    dve.wait_ge(pv_ok, n2 + (4 + 1))
                    dve.tensor_scalar(o_mla[:, bass.ds(n, 1), :], out_bank[0][:, 0:KVL].unsqueeze(1), inverse[:, b, 0:1], None, ALU.mult).then_inc(mla_taken, 1)
                    dve.wait_ge(pv_ok, n2 + (4 + 2))
                    dve.wait_ge(folded_ok, n + 1)
                    dve.tensor_tensor(picked[:, :, :], o_ps[:, :].rearrange("p (h d) -> p h d", h=H), head_pick.unsqueeze(2).broadcast_to([P, H, 64]), ALU.mult).then_inc(fox_taken, 1)
                    dve.wait_ge(fox_taken, n + 2)
                    dve.tensor_reduce(folded[:, :], picked[:, :, :].rearrange("p h d -> p d h"), axis=AX.X, op=ALU.add).then_inc(picked_ok, 1)
                    dve.wait_ge(picked_ok, n + 1)
                    dve.tensor_scalar(o_fox[:, bass.ds(n, 1), :], folded[:, :].unsqueeze(1), inverse[:, b, 1:2], None, ALU.mult).then_inc(folded_ok, 1)

                def stream(i, b, follows):
                    if follows:
                        take_flips(dve, dve.tensor_copy, 1, i + b, 1 - b)
                        maxima(i + b, 1 - b)
                    outputs(i, b)

                take_flips(dve, dve.tensor_copy, 1, 0, 0)
                maxima(0, 0)
                with dve.Fori(0, DECB // 2 - 1) as i:
                    for b in range(2):
                        stream(i, b, True)
                for b in range(2):
                    stream(DECB // 2 - 1, b, b == 0)

            @block.tensor
            def _(pe):
                pe.sem_inc(flip_ready, 2 * FLIPS)
                pe.sem_inc(kept, 2)
                pe.sem_inc(s_ready, 4)
                pe.sem_inc(pv_ok, 4)
                for free in (mla_taken, fox_taken, folded_ok):
                    pe.sem_inc(free, 1)

                def transpose_keys(i2, b):
                    pe.wait_ge(keys_in[b], i2 * (16 * LOADS) + 16 * LOADS)
                    for g, ((parts, _, _), _) in enumerate(flips):
                        G = flip_number(b, g)
                        if not isinstance(i2, int) or G // 2 or i2:
                            pe.wait_ge(flip_ok[G % 2], i2 * FLIPS + G // 2)
                        for r in range(CK):
                            last = pe.transpose(flip[0:parts, G % 2, r * P:r * P + P], flip_rows(b, g, r), ident[:, :])
                        last.then_inc(flip_ready, 1)

                def product(out, pairs, more):
                    for c, (w, x) in enumerate(pairs):
                        last = pe.matmul(out, w, x, start=(c == 0), stop=(c == len(pairs) - 1 and not more))
                    return last

                def score(i2, b, last_stream=None):
                    n = i2 * 2 + b
                    new = bass.ds(n * NEW, NEW)
                    def copied(groups):
                        for e in range(2):
                            pe.wait_ge(flip_ok[e], i2 * FLIPS + (flip_number(b, groups) + 1 - e) // 2)

                    pe.wait_ge(staged, n * STAGES + STAGES)
                    copied(KC + 1)
                    product(cached_part[0], [(qc[b][:, c, :], ckvT[:, c, :]) for c in range(KC)] + [(qr[b][:, :], krT[:, :])], False)
                    if last_stream is not None:
                        pe.wait_ge(pt_ok, last_stream + 1)
                    product(new_part[1], [(qf[b][:, c, :], s["knT"][:, c, new]) for c in range(4)] + [(qa[b][:, :], s["aug_r"][:, PAST:KEYS])], True)
                    pe.matmul(new_part[1], ident_bf[:, :], mask_bf, start=False, stop=True)
                    product(new_part[0], [(qc[b][:, c, :], s["cnT"][:, c, new]) for c in range(KC)] + [(qr[b][:, :], s["krnT"][:, new])], False).then_inc(s_ready, 1)
                    copied(FLIPS)
                    product(cached_part[1], [(qf[b][:, c, :], fkT[:, c, :]) for c in range(4)] + [(qa[b][:, :], s["aug_r"][:, 0:PAST].rearrange("q (p r) -> q r p", r=CK))], False).then_inc(s_ready, 1)

                def stream(i, b, follows):
                    n2 = i * 4 + 2 * b
                    n = i * 2 + b
                    pe.wait_ge(mla_taken, n + 1)
                    for m in range(2):
                        pe.wait_ge(exp_ok, n2 + (m + 1))
                        for r in range(CK):
                            last = pe.transpose(pT_ps[:, m, r * P:r * P + P], p_cached[m][:, r * P:r * P + P], ident[:, :])
                        if m == 0:
                            last.then_inc(pt_ready, 1)
                    for m in range(2):
                        last = pe.transpose(pTn_ps[m], p_new[m], ident[:, :])
                    last.then_inc(pt_ready, 1)
                    if follows:
                        transpose_keys(i + b, 1 - b)
                        score(i + b, 1 - b, n2)
                    pe.wait_ge(values_in[b], i * (16 * LOADS) + 16 * LOADS)
                    pe.wait_ge(kept, i * 2 + (b + 3))
                    for m in range(2):
                        pe.wait_ge(pt_ok, n2 + 2)
                        if m == 1:
                            pe.wait_ge(fox_taken, n + 1)
                        rows, new_rows, w = (ckv[b], cn[b], KVL) if m == 0 else (fv[b], vn[b], FW)
                        for r in range(CK):
                            pe.matmul(out_bank[m][:, 0:w], pT[m][:, r, :], rows[:, r, :], start=(r == 0), stop=False)
                        pe.matmul(out_bank[m][:, 0:w], pTn[m][:, :], new_rows[:, :], start=False, stop=True).then_inc(pv_ok, 1)

                transpose_keys(0, 0)
                score(0, 0)
                with pe.Fori(0, DECB // 2 - 1) as i:
                    for b in range(2):
                        stream(i, b, True)
                for b in range(2):
                    stream(DECB // 2 - 1, b, b == 0)

        with Tools(nc, "back") as e:
            olT = fk[0][:, :, :].rearrange("p r n -> p (r n)").rearrange("p (c h b t) -> p c h b t", c=KC, h=H, t=NEW)
            ofT = fk[1][0:64, :, :].rearrange("p r n -> p (r n)")[:, 0:H * P].rearrange("p (h b t) -> p h b t", h=H, t=NEW)
            hop, hopped, rows_ok = e.sem("hop"), e.sem("hopped"), e.sem("rows_ok")
            banks = [flip[:, 0, :], flip[:, 1, :], scores[:, 0:HALF], scores[:, HALF:2 * HALF]]
            mla_out, fox_out = pT_ps[:, 0, :], o_ps[:, :]
            units = [(b, m) for b in range(DECB) for m in range(2)]
            with e.block() as block:
                @block.sync
                def _(sp):
                    load_fox_rows(sp, fox_rows, prompt_rows, prompt_loaded)

                @block.tensor
                def _(pe):
                    for n, (b, m) in enumerate(units):
                        if n >= 4:
                            pe.wait_ge(hopped, n - 3)
                        if m == 0:
                            for c in range(KC):
                                last = pe.transpose(banks[n % 4][:, c * P:c * P + P], o_mla[:, b, c * P:c * P + P], ident[:, :])
                        else:
                            last = pe.transpose(banks[n % 4][0:64, 0:P], o_fox[:, b, :], ident[:, :])
                        last.then_inc(hop, 1)
                    pe.wait_ge(hopped, len(units))
                    for h in range(H):
                        for c in range(KC):
                            pe.matmul(mla_out[:, h * VD:h * VD + VD], olT[:, c, h, :, :].rearrange("p b t -> p (b t)"), s["w_kv"][:, c, h * P + NOPE:h * P + P],
                                      start=(c == 0), stop=(c == KC - 1))
                    for h in range(H):
                        last = pe.transpose(fox_out[:, h * 64:h * 64 + 64], ofT[:, h, :, :].rearrange("p b t -> p (b t)"), ident[0:64, 0:64])
                    last.then_inc(hop, 1)

                @block.vector
                def _(dve):
                    for n, (b, m) in enumerate(units):
                        dve.wait_ge(hop, n + 1)
                        if m == 0:
                            dve.tensor_copy(olT[:, :, :, b, :], banks[n % 4][:, 0:KVL].rearrange("p (c h t) -> p c h t", c=KC, t=NEW)).then_inc(hopped, 1)
                        else:
                            dve.tensor_copy(ofT[:, :, b, :], banks[n % 4][0:64, 0:P].rearrange("p (h t) -> p h t", t=NEW)).then_inc(hopped, 1)
                    dve.wait_ge(hop, len(units) + 1)
                    dve.tensor_copy(o_rows[:, PT, 0:HALF], mla_out)
                    dve.tensor_copy(o_rows[:, PT, HALF:D], fox_out)


RAW = 4


def load_w_out(sp, w_out, raw, c, w_at):
    sp.dma_start(raw[:, c % RAW, :], w_out.rearrange("(k p) n -> p k n", p=P)[:, c, :]).then_inc(w_at[c % RAW], 16)


def output_projection(nc, tag, ident, w_out, raw, raw_at, w_at, xT_hi, xT_lo, acc, post, pre, load_next):
    with Tools(nc, tag) as k:
        hi = k.sb("hi", [P, KD, D], F32R)
        lo = k.sb("lo", [P, KD, D], F32R)
        assert nc.sbuf_base == raw_at
        k.sb("raw_place", [P, RAW, D])
        more_at = nc.sbuf_base
        k.sb("more", [P, 4, D])
        prod = k.ps("prod", [P, 2, HALF])
        flip = k.ps("flip", [P, 2, HALF])
        leave_flip = k.ps("leave_flip", [P, 4, HALF])
        w_lo = [k.sem(f"w_lo_{n}") for n in ("pool", "dve")]
        w_hi, flipped, hi_ok, lo_ok, made, taken = [k.sem(n) for n in ("w_hi", "flipped", "hi_ok", "lo_ok", "made", "taken")]
        AFTER = 3

        def row_made(act, t):
            act.wait_ge(taken, 2 * t + 2)

        leave = Boundary(k, "exit", acc, row_made, ident, xT_hi, xT_lo, post, pre,
                         [Region(nc, tag, at, 2 * D * 4) for at in (more_at, more_at + 2 * D * 4, raw_at, raw_at + 2 * D * 4)],
                         [leave_flip[:, n, :] for n in range(4)])

        def split_weight(eng, c):
            eng.wait_ge(w_hi, c + 1)
            eng.tensor_tensor(lo[:, c, :], raw[:, c % RAW, :], plain(hi[:, c, :]), ALU.subtract).then_inc(w_lo[c % 2], 1)

        with k.block() as block:
            @block.sync
            def _(sp):
                for c in range(RAW, KD):
                    sp.wait_ge(w_lo[c % 2], (c - RAW) // 2 + 1)
                    load_w_out(sp, w_out, raw, c, w_at)
                leave.load_first(sp)
                leave.load_and_store(sp, TT - 2)
                sp.wait_ge(made, 2 * TT)
                load_next(sp)
                leave.load_and_store(sp, TT, TT - 2)

            @block.scalar
            def _(act):
                def split_high(t):
                    for h in range(2):
                        act.wait_ge(flipped, 2 * t + h + 1)
                        act.activation(xT_hi[:, 4 * h:4 * h + 4, t * P:t * P + P], flip[:, h, :].rearrange("p (k n) -> p k n", k=4),
                                       ACT.Copy).then_inc(hi_ok, 1)

                split_high(0)
                for c in range(KD):
                    act.wait_ge(w_at[c % RAW], 16 * (c // RAW + 1))
                    act.activation(hi[:, c, :], raw[:, c % RAW, :], ACT.Copy).then_inc(w_hi, 1)
                split_high(1)
                for s in range(leave.steps):
                    leave.act(act, s)
                    if s + 2 < TT:
                        split_high(s + 2)

            @block.gpsimd
            def _(pool):
                for c in range(0, KD, 2):
                    split_weight(pool, c)
                for t in range(TT):
                    leave.pool(pool, t)

            @block.vector
            def _(dve):
                def split_low(t):
                    for h in range(2):
                        dve.wait_ge(hi_ok, 2 * t + h + 1)
                        dve.tensor_tensor(xT_lo[:, 4 * h:4 * h + 4, t * P:t * P + P], flip[:, h, :].rearrange("p (k n) -> p k n", k=4),
                                          plain(xT_hi[:, 4 * h:4 * h + 4, t * P:t * P + P]), ALU.subtract).then_inc(lo_ok, 1)

                split_low(0)
                for c in range(1, KD, 2):
                    split_weight(dve, c)
                split_low(1)
                for s in range(leave.steps):
                    for h in range(2 if s < TT else 0):
                        dve.wait_ge(made, 2 * s + h + 1)
                        dve.tensor_copy(acc[:, s, h * HALF:h * HALF + HALF], prod[:, h, :]).then_inc(taken, 1)
                    leave.dve(dve, s)
                    if s + 2 < TT:
                        split_low(s + 2)

            @block.tensor
            def _(pe):
                def turn(t):
                    for h in range(2):
                        if t:
                            pe.wait_ge(lo_ok, 2 * (t - 1) + h + 1)
                        for c in range(4):
                            kk = 4 * h + c
                            last = pe.transpose(flip[:, h, c * P:c * P + P], acc[:, t, kk * P:kk * P + P], ident[:, :])
                        last.then_inc(flipped, 1)

                turn(0)
                turn(1)
                for t in range(TT + AFTER):
                    if t < TT:
                        pe.wait_ge(lo_ok, 2 * t + 2)
                        for h in range(2):
                            if t:
                                pe.wait_ge(taken, 2 * (t - 1) + h + 1)
                            for c in range(KD):
                                if t == 0 and h == 0:
                                    pe.wait_ge(w_lo[c % 2], c // 2 + 1)
                                last = split_product(pe, prod[:, h, :], xT_hi[:, c, t * P:t * P + P], xT_lo[:, c, t * P:t * P + P],
                                                     hi[:, c, h * HALF:h * HALF + HALF], lo[:, c, h * HALF:h * HALF + HALF], c == 0, c == KD - 1)
                            last.then_inc(made, 1)
                    if t + 2 < TT:
                        turn(t + 2)
                    if t >= AFTER:
                        leave.pe(pe, t - AFTER)


def layer(nc, x_prompt, x_sample, cache_ckv, cache_krope, cache_fk, cache_fv, cache_logf, g1_pre, g1_post, w1_gu, w1_down,
          gm_pre, gm_post, w_in, b_forget, g_q, w_q_up, g_kv, w_kv_up, w_out, g2_pre, g2_post, w2_gu, w2_down,
          identity, masks, triangle, pick, select, cos_sin, y, ckv_out, krope_out, fox_rows, logf_out):
    h1 = nc.dram_tensor("h1", [T, D], F32, kind="Internal").ap()
    h2 = nc.dram_tensor("h2", [T, D], F32, kind="Internal").ap()

    def x_rows(t):
        return x_prompt[t * P:t * P + P, :] if t < PT else x_sample

    def tile_of(a):
        return lambda t: a[t * P:t * P + P, :]

    with Tools(nc, "all") as k:
        ident = k.sb("ident", [P, P])
        ident_bf = k.sb("ident_bf", [P, P], BF16)
        mask_bf = k.sb("mask_bf", [P, 2 * P + NEW], BF16)
        tri, ones, head_pick = k.sb("tri", [P, P]), k.sb("ones", [P, P]), k.sb("head_pick", [P, H])
        consts_in = k.sem("consts_in")
        with Tools(nc, "consts") as c:
            wide = c.sb("wide", [P, 2 * P + NEW])
            with c.block() as block:
                @block.sync
                def _(sp):
                    sp.dma_start(ident[:, :], identity).then_inc(consts_in, 16)
                    sp.dma_start(wide[:, :], masks).then_inc(consts_in, 16)
                    sp.dma_start(tri[:, :], triangle).then_inc(consts_in, 16)
                    sp.dma_start(head_pick[:, :], pick).then_inc(consts_in, 16)

                @block.vector
                def _(dve):
                    dve.wait_ge(consts_in, 64)
                    dve.memset(ones[:, :], 1.0)
                    dve.tensor_copy(ident_bf[:, :], ident[:, :])
                    dve.tensor_copy(mask_bf[:, :], wide[:, :])

        acc = k.sb("acc", [P, TT, D])
        xT_at = nc.sbuf_base
        xT_hi, xT_lo = k.sb("xT_hi", [P, KD, T], F32R), k.sb("xT_lo", [P, KD, T], F32R)

        after_xT = nc.sbuf_base
        piece = KD * 2 * P * 4

        gu_raw = [nc.alloc_sbuf_tensor_at(f"gu_raw{j}", [P, KD, 2 * P], F32, offset=after_xT + j * piece) for j in range(FB)]
        in_raw_at = after_xT + 2 * FB * piece
        in_raw = [nc.alloc_sbuf_tensor_at(f"in_raw{h}", [P, KH, HALF], F32, offset=in_raw_at + h * KH * HALF * 4) for h in range(2)]
        w_out_raw_at = after_xT + 2 * KD * D * 4
        w_out_raw = nc.alloc_sbuf_tensor_at("w_out_raw", [P, RAW, D], F32, offset=w_out_raw_at)
        w_out_at = [k.sem(f"w_out_at{n}") for n in range(RAW)]
        gu_in = [[k.sem(f"gu_in{n}{j}") for j in range(FB)] for n in range(2)]
        in_at = [k.sem(f"in_at{h}") for h in range(2)]

        def load_w_in(sp):
            load_in_group(sp, in_raw, w_in, [(FOX_AT, FW)], in_at)

        def load_w2(sp):
            for j in range(FB):
                load_gate_up(sp, gu_raw[j], w2_gu, bass.ds(j, 1), gu_in[1][j])

        def load_first_w_out(sp):
            for c in range(RAW):
                load_w_out(sp, w_out, w_out_raw, c, w_out_at)

        def spare(tag):
            return Region(nc, tag, xT_at, 2 * KD * T * 4)

        feed_forward(nc, "ffn1", ident, acc, xT_hi, xT_lo, w1_gu, w1_down, gu_raw, gu_in[0], x_rows, g1_pre,
                     (g1_post, 0.5, x_rows, tile_of(h1)), gm_pre, load_w_in)

        with Tools(nc, "mix") as m:
            fox_loaded = m.sem("fox_loaded")
            logf, krope = m.sb("logf", [P, TT, H]), m.sb("krope", [P, TT, ROPE])
            with Tools(nc, "lat") as l:
                cq, ckv, gate = l.sb("cq", [P, TT, QL]), l.sb("ckv", [P, TT, KVL + ROPE]), l.sb("gate", [P, TT, H])
                input_projection(nc, "inp", w_in, in_raw, in_raw_at, in_at, xT_hi, xT_lo, fox_rows, cq, ckv, gate)
                up = spare("up_rows")
                kv_rows, q_rows = up.take("kv_rows", [P, PT, D]), up.take("q_rows", [P, TT, H * QW])
                latents(nc, "latents", ident, cq, ckv, gate, g_q, g_kv, b_forget, w_q_up, w_kv_up, cos_sin, q_rows, kv_rows, up,
                        krope, logf, ckv_out, krope_out, logf_out)
            own = {}
            places = (
                (Region(nc, "dec_tail", xT_at + KD * T * 8 - KC * D * 4, KC * D * 4), dict(w_kv=[P, KC, D])),
                (Region(nc, "dec_past", xT_at + (PT * D + TT * H * QW) * 4, KD * T * 8 - (PT * D + TT * H * QW + KC * D) * 4),
                 dict(logs_in=[P, DECB, CK, H], new_logs=[NEW, DECB, H], cn=[P, KVL], kn=[P, ROPE], fq=[P, FW])),
                (Region(nc, "dec_high", nc.sbuf_usable_end // 32 * 32 - 2 * CK * (KVL + ROPE + FW) * 4 - FW * 4, 2 * CK * (KVL + ROPE + FW) * 4 + FW * 4),
                 dict(fk=[P, FW], **{f"{n}{b}": [P, CK, w] for b in range(2) for n, w in (("ckv_in", KVL), ("kr", ROPE), ("fk", FW))})),
                (Region(nc, "dec_x", xT_at, (PT * D + TT * H * QW) * 4), dict(
                    qbd=[P, 4, DECB, P], qcT=[P, KC, DECB, H, NEW], aug_l=[P, DECB, P], knT=[P, 4, P], cnT=[P, KC, P], krnT=[ROPE, P],
                    qrT=[ROPE, DECB, H, NEW], aug_r=[P, KEYS], l_new=[P, NEW], fv0=[P, CK, FW], fv1=[P, CK, FW])))
            for region, parts in places:
                own |= {name: region.take(name, shape) for name, shape in parts.items()}
            setup_in = m.sem("setup_in")
            keys_in = [m.sem(f"keys_in{b}") for b in range(2)]

            def load_first_keys(sp):
                for b in range(2):
                    load_keys(sp, bass.ds(b, 1), own[f"kr{b}"], own[f"fk{b}"], cache_krope, cache_fk, keys_in[b])
                    sp.dma_start(own[f"ckv_in{b}"][:, :, :], cache_rows(cache_ckv, bass.ds(b, 1))).then_inc(keys_in[b], 16)

            mla_prompt(nc, ident, ident_bf, mask_bf[:, 0:P], q_rows, kv_rows, krope, acc,
                       lambda sp: load_setup_rows(sp, cache_logf, fox_rows, ckv_out, krope_out, w_kv_up, logf_out, own, setup_in))
            with Tools(nc, "dec_all") as d:
                q_sample = d.sb("q_sample", [P, H * QW])
                with d.block() as block:
                    @block.vector
                    def _(dve):
                        dve.tensor_copy(q_sample[:, :], q_rows[:, PT, :])
                fox_x = Region(nc, "fox_x", xT_at, 3 * PT * FW * 4)
                fox_prompt_rows = [fox_x.take(f"rows{n}", [P, PT, FW]) for n in range(3)]
                sample_setup(nc, ident, q_sample, select, setup_in, load_first_keys, own)
                sample_attention(nc, ident, ident_bf, mask_bf[:, 2 * P:2 * P + NEW], head_pick[:, :], own, cache_ckv, cache_krope, cache_fk, cache_fv, fox_rows, ckv_out, acc, fox_prompt_rows, fox_loaded, keys_in)
            fox_prompt(nc, ident, ident_bf, mask_bf[:, P:2 * P], tri[:, :], ones[:, :], logf, fox_prompt_rows, fox_loaded, acc, load_first_w_out)

        output_projection(nc, "outp", ident, w_out, w_out_raw, w_out_raw_at, w_out_at, xT_hi, xT_lo, acc, (gm_post, 1.0, tile_of(h1), tile_of(h2)), g2_pre, load_w2)

        feed_forward(nc, "ffn2", ident, acc, xT_hi, xT_lo, w2_gu, w2_down, gu_raw, gu_in[1], None, None,
                     (g2_post, 0.5, tile_of(h2), tile_of(y)), None, lambda sp: None)


def kernel(**inputs):
    import numpy as _np
    import concourse.bacc as _bacc
    from concourse import mybir as _mybir
    from concourse.bass_utils import run_bass_kernel_spmd as _run

    f32 = _np.float32
    shapes = dict(
        x_prompt=(SEQ, D), x_sample=(P, D), cache_mla_ckv=(DECB, PAST, KVL), cache_mla_krope=(DECB, PAST, ROPE), cache_fox_k=(DECB, PAST, FW),
        cache_fox_v=(DECB, PAST, FW), cache_fox_logf=(DECB, PAST, H), g_ffn1_pre=(D,), g_ffn1_post=(D,), w_ffn1_gu=(D, 2 * FF), w_ffn1_down=(FF, D),
        g_mix_pre=(D,), g_mix_post=(D,), w_in=(D, IN_COLS), b_forget=(H,), g_q_latent=(QL,), w_q_up=(QL, H * QW), g_kv_latent=(KVL,), w_kv_up=(KVL, D),
        w_out=(D, D), g_ffn2_pre=(D,), g_ffn2_post=(D,), w_ffn2_gu=(D, 2 * FF), w_ffn2_down=(FF, D))
    arrays = {n: _np.ascontiguousarray(inputs[n]).reshape(s) for n, s in shapes.items()}
    tile = _np.arange(P)
    hide = f32(-1e30)
    masks = _np.zeros((P, 2 * P + NEW), f32)
    masks[:, 0:P][tile[None, :] // 64 > tile[:, None] // 64] = hide
    masks[:, P:2 * P][tile[None, :] > tile[:, None]] = hide
    masks[:, 2 * P:][_np.arange(NEW)[None, :] > tile[:, None] % NEW] = hide
    select = _np.zeros((BH, DECB, P), f32)
    for b in range(DECB):
        for h in range(H):
            select[b * H + h, b, h * NEW:h * NEW + NEW] = 1
    pos = _np.concatenate([_np.arange(SEQ), _np.tile(PAST + _np.arange(NEW), DECB)]).astype(f32)
    freqs = f32(10000.0) ** (-_np.arange(ROPE // 2, dtype=f32) / f32(ROPE // 2))
    angle = pos[:, None] * freqs[None, :].astype(f32)
    cos_sin = _np.stack([_np.cos(angle), _np.sin(angle)], 1).astype(f32).reshape(TT, P, 2, ROPE // 2).transpose(1, 0, 2, 3)
    arrays |= dict(identity=_np.eye(P, dtype=f32), masks=masks, triangle=_np.triu(_np.ones((P, P), f32)),
                   pick=(tile[:, None] // NEW == _np.arange(H)[None, :]).astype(f32), select=select, cos_sin=_np.ascontiguousarray(cos_sin))
    outs = dict(y=(T, D), ckv=(T, KVL), krope=(T, ROPE), fox=(3, T, FW), logf=(T, H))

    nc = _bacc.Bacc("TRN2", target_bir_lowering=False, num_devices=1)
    args = [nc.dram_tensor(f"in_{n}", a.shape, _mybir.dt.from_np(a.dtype), kind="ExternalInput").ap() for n, a in arrays.items()]
    args += [nc.dram_tensor(f"out_{n}", s, _mybir.dt.float32, kind="ExternalOutput").ap() for n, s in outs.items()]
    layer(nc, *args)
    r = _run(nc, [{f"in_{n}": a for n, a in arrays.items()}], core_ids=[0]).results[0]
    y, ckv, krope, fox, logf = (r[f"out_{n}"] for n in outs)
    results = [y[:SEQ].reshape(1, SEQ, D), y[SEQ:].reshape(DECB, DECT, D)]
    for rows, lead in ((slice(0, SEQ), (1, 1, SEQ)), (slice(SEQ, T), (1, DECB, DECT))):
        results += [ckv[rows].reshape(*lead, KVL), krope[rows].reshape(*lead, ROPE), fox[1, rows].reshape(*lead, H, 64), fox[2, rows].reshape(*lead, H, 64),
                    logf[rows].reshape(*lead, H)]
    return tuple(results)
```
